# Optimizing a Trainium2 kernel written in Bass

```python
import math
import jax, jax.numpy as jnp
from jax import lax
import numpy as np

D_MODEL = 1024
BATCH = 1
SEQ = 1024
DEPTH = 1

DA_HEADS = 8
DA_HEAD_DIM = 64
DA_V_DIM = 2 * DA_HEAD_DIM
DA_QK_WIDTH = DA_HEADS * 2 * DA_HEAD_DIM
DA_WIDTH = DA_HEADS * DA_V_DIM
ROPE_DIM = DA_HEAD_DIM // 4
ROPE_THETA = 500000.0
Q_BLOCK = 128
ML_HEADS = 8
ML_QK_DIM = 64
ML_V_DIM = 128
ML_QK_WIDTH = ML_HEADS * ML_QK_DIM
ML_V_WIDTH = ML_HEADS * ML_V_DIM
CONV_WIDTH = 4
CHUNK = 64
N_BRANCH = 2
D_FF = 4 * D_MODEL
EPS = 1e-6
SPLIT_SIZES = (DA_QK_WIDTH, DA_QK_WIDTH, DA_WIDTH,
               ML_QK_WIDTH, ML_QK_WIDTH, ML_V_WIDTH, ML_HEADS, ML_HEADS, ML_V_WIDTH,
               N_BRANCH * D_MODEL)
D_IN = sum(SPLIT_SIZES)

kernel_name = "hybrid_diffattn_mlstm_gated_block"

def rms_norm(x, w):
    x32 = x.astype(jnp.float32)
    y = x32 * lax.rsqrt(jnp.mean(x32 * x32, axis=-1, keepdims=True) + EPS)
    return (y * w.astype(jnp.float32)).astype(x.dtype)

def rope_tables(positions):
    inv = ROPE_THETA ** (-jnp.arange(0, ROPE_DIM, 2, dtype=jnp.float32) / ROPE_DIM)
    ang = positions.astype(jnp.float32)[..., None] * inv
    return jnp.cos(ang), jnp.sin(ang)

def apply_partial_rope(x, cos, sin):
    half = ROPE_DIM // 2
    xr = x[..., :ROPE_DIM].astype(jnp.float32)
    x1, x2 = xr[..., :half], xr[..., half:]
    c = cos[:, :, None, None, :]
    s = sin[:, :, None, None, :]
    rot = jnp.concatenate([x1 * c - x2 * s, x2 * c + x1 * s], axis=-1)
    return jnp.concatenate([rot.astype(x.dtype), x[..., ROPE_DIM:]], axis=-1)

def diff_attention(q, k, v, lam, cos, sin):
    B, S = q.shape[0], q.shape[1]
    H, d, dv = DA_HEADS, DA_HEAD_DIM, DA_V_DIM
    q = apply_partial_rope(q, cos, sin).astype(jnp.float32) * (d ** -0.5)
    k = apply_partial_rope(k, cos, sin).astype(jnp.float32)
    q = q.transpose(0, 2, 3, 1, 4)
    k = k.transpose(0, 2, 3, 1, 4)
    v32 = v.astype(jnp.float32).transpose(0, 2, 1, 3)
    nblk = S // Q_BLOCK
    qb = jnp.moveaxis(q.reshape(B, H, 2, nblk, Q_BLOCK, d), 3, 0)
    kpos = jnp.arange(S)

    def block(args):
        q_blk, j = args
        s = jnp.einsum('bhcqd,bhckd->bhcqk', q_blk, k)
        qpos = j * Q_BLOCK + jnp.arange(Q_BLOCK)
        mask = kpos[None, :] <= qpos[:, None]
        p = jax.nn.softmax(jnp.where(mask, s, -jnp.inf), axis=-1)
        a = p[:, :, 0] - lam * p[:, :, 1]
        return jnp.einsum('bhqk,bhkv->bhqv', a, v32)

    o = lax.map(block, (qb, jnp.arange(nblk)))
    o = jnp.moveaxis(o, 0, 2).reshape(B, H, S, dv)
    return o.transpose(0, 2, 1, 3)

def causal_dwconv(u, w, b):
    S = u.shape[1]
    up = jnp.pad(u, ((0, 0), (CONV_WIDTH - 1, 0), (0, 0)))
    out = b
    for j in range(CONV_WIDTH):
        out = out + up[:, j:j + S] * w[j]
    return out

def mlstm_chunkwise(q, k, v, i_pre, f_pre):
    B, H, S, dk = q.shape
    dv = v.shape[-1]
    L = CHUNK
    NC = S // L
    q = q * (dk ** -0.5)
    logf = jax.nn.log_sigmoid(f_pre)

    def chunks(a):
        return jnp.moveaxis(a.reshape((B, H, NC, L) + a.shape[3:]), 2, 0)

    qc, kc, vc, ic = chunks(q), chunks(k), chunks(v), chunks(i_pre)
    bc = jnp.cumsum(chunks(logf), axis=-1)
    tri = jnp.tril(jnp.ones((L, L), dtype=bool))

    def step(carry, inp):
        C, n, m = carry
        qb, kb, vb, ib, bb = inp
        D = jnp.where(tri, bb[..., :, None] - bb[..., None, :] + ib[..., None, :], -jnp.inf)
        m_inter = bb + m[..., None]
        m_t = jnp.maximum(jnp.max(D, axis=-1), m_inter)
        dexp = jnp.exp(D - m_t[..., None])
        inter = jnp.exp(m_inter - m_t)
        s = jnp.einsum('bhtd,bhsd->bhts', qb, kb) * dexp
        num = jnp.einsum('bhts,bhsv->bhtv', s, vb) + inter[..., None] * jnp.einsum('bhtd,bhdv->bhtv', qb, C)
        den = jnp.sum(s, axis=-1) + inter * jnp.einsum('bhtd,bhd->bht', qb, n)
        h = num / jnp.maximum(jnp.abs(den), jnp.exp(-m_t))[..., None]
        b_last = bb[..., -1]
        w_log = b_last[..., None] - bb + ib
        m_new = jnp.maximum(b_last + m, jnp.max(w_log, axis=-1))
        decay = jnp.exp(b_last + m - m_new)
        ws = jnp.exp(w_log - m_new[..., None])
        C_new = decay[..., None, None] * C + jnp.einsum('bhs,bhsd,bhsv->bhdv', ws, kb, vb)
        n_new = decay[..., None] * n + jnp.einsum('bhs,bhsd->bhd', ws, kb)
        return (C_new, n_new, m_new), h

    init = (jnp.zeros((B, H, dk, dv), jnp.float32), jnp.zeros((B, H, dk), jnp.float32),
            jnp.zeros((B, H), jnp.float32))
    _, hs = lax.scan(step, init, (qc, kc, vc, ic, bc))
    return jnp.moveaxis(hs, 0, 2).reshape(B, H, S, dv)

def setup_inputs(seed: int = 0) -> dict:
    key = jax.random.key(seed)
    ks = jax.random.split(key, 20)
    f32 = jnp.float32
    nrm = lambda k, shape, scale: jax.random.normal(k, shape, f32) * scale
    x = jax.random.normal(ks[0], (BATCH, SEQ, D_MODEL), f32)
    positions = jnp.broadcast_to(jnp.arange(SEQ, dtype=jnp.int32), (BATCH, SEQ))
    gate_b_i = nrm(ks[1], (DEPTH, ML_HEADS), 0.1)
    gate_b_f = jnp.linspace(3.0, 6.0, ML_HEADS, dtype=f32)[None, :] + nrm(ks[2], (DEPTH, ML_HEADS), 0.1)
    return {
        "x": x,
        "positions": positions,
        "norm_mix_w": 1.0 + nrm(ks[3], (DEPTH, D_MODEL), 0.02),
        "w_in": nrm(ks[4], (DEPTH, D_MODEL, D_IN), D_MODEL ** -0.5),
        "ml_gate_b": jnp.concatenate([gate_b_i, gate_b_f], axis=-1),
        "conv_w": nrm(ks[5], (DEPTH, CONV_WIDTH, 2 * ML_QK_WIDTH), CONV_WIDTH ** -0.5),
        "conv_b": nrm(ks[6], (DEPTH, 2 * ML_QK_WIDTH), 0.01),
        "da_lambda": nrm(ks[7], (DEPTH, 4, DA_HEAD_DIM), 0.1),
        "da_subln_w": 1.0 + nrm(ks[8], (DEPTH, DA_V_DIM), 0.02),
        "ml_norm_w": 1.0 + nrm(ks[9], (DEPTH, ML_V_WIDTH), 0.02),
        "w_proj_a": nrm(ks[10], (DEPTH, DA_WIDTH, D_MODEL), DA_WIDTH ** -0.5),
        "w_proj_b": nrm(ks[11], (DEPTH, ML_V_WIDTH, D_MODEL), ML_V_WIDTH ** -0.5),
        "w_out": nrm(ks[12], (DEPTH, D_MODEL, D_MODEL), D_MODEL ** -0.5),
        "norm_ffn_w": 1.0 + nrm(ks[13], (DEPTH, D_MODEL), 0.02),
        "w_ff1": nrm(ks[14], (DEPTH, D_MODEL, D_FF), D_MODEL ** -0.5),
        "w_ff2": nrm(ks[15], (DEPTH, D_FF, D_MODEL), D_FF ** -0.5),
        "final_norm_w": 1.0 + nrm(ks[16], (D_MODEL,), 0.02),
    }

def reference(x, positions, norm_mix_w, w_in, ml_gate_b, conv_w, conv_b, da_lambda,
              da_subln_w, ml_norm_w, w_proj_a, w_proj_b, w_out, norm_ffn_w, w_ff1,
              w_ff2, final_norm_w):
    B, S, _ = x.shape
    cos, sin = rope_tables(positions)
    split_idx = [int(c) for c in np.cumsum(SPLIT_SIZES)[:-1]]
    h = x
    for l in range(DEPTH):
        lambda_init = 0.8 - 0.6 * math.exp(-0.3 * l)
        xn = rms_norm(h, norm_mix_w[l])
        proj = jnp.einsum('bsd,de->bse', xn, w_in[l])
        (da_q, da_k, da_v, ml_q, ml_k, ml_v, ml_i, ml_f, ml_o, gate_pre) = jnp.split(proj, split_idx, axis=-1)

        lam_p = da_lambda[l].astype(jnp.float32)
        lam = (jnp.exp(jnp.sum(lam_p[0] * lam_p[1])) - jnp.exp(jnp.sum(lam_p[2] * lam_p[3]))
               + lambda_init)
        qa = da_q.reshape(B, S, DA_HEADS, 2, DA_HEAD_DIM)
        ka = da_k.reshape(B, S, DA_HEADS, 2, DA_HEAD_DIM)
        va = da_v.reshape(B, S, DA_HEADS, DA_V_DIM)
        oa = diff_attention(qa, ka, va, lam, cos, sin)
        oa = rms_norm(oa, da_subln_w[l]) * (1.0 - lambda_init)
        ya = jnp.einsum('bse,ed->bsd', oa.reshape(B, S, DA_WIDTH).astype(x.dtype), w_proj_a[l])

        qk = jax.nn.silu(causal_dwconv(jnp.concatenate([ml_q, ml_k], axis=-1), conv_w[l], conv_b[l]))
        qm = qk[..., :ML_QK_WIDTH].reshape(B, S, ML_HEADS, ML_QK_DIM).transpose(0, 2, 1, 3)
        km = qk[..., ML_QK_WIDTH:].reshape(B, S, ML_HEADS, ML_QK_DIM).transpose(0, 2, 1, 3)
        vm = ml_v.reshape(B, S, ML_HEADS, ML_V_DIM).transpose(0, 2, 1, 3)
        i_pre = (ml_i + ml_gate_b[l, :ML_HEADS]).transpose(0, 2, 1)
        f_pre = (ml_f + ml_gate_b[l, ML_HEADS:]).transpose(0, 2, 1)
        hm = mlstm_chunkwise(qm.astype(jnp.float32), km.astype(jnp.float32), vm.astype(jnp.float32),
                             i_pre.astype(jnp.float32), f_pre.astype(jnp.float32))
        hm = hm.transpose(0, 2, 1, 3)
        hm = rms_norm(hm, ml_norm_w[l].reshape(ML_HEADS, ML_V_DIM)).reshape(B, S, ML_V_WIDTH)
        ob = (jax.nn.sigmoid(ml_o.astype(jnp.float32)) * hm).astype(x.dtype)
        yb = jnp.einsum('bse,ed->bsd', ob, w_proj_b[l])

        g = jax.nn.sigmoid(gate_pre.astype(jnp.float32)).reshape(B, S, N_BRANCH, D_MODEL).astype(x.dtype)
        merged = g[:, :, 0] * ya + g[:, :, 1] * yb
        h = h + jnp.einsum('bsd,de->bse', merged, w_out[l])

        hn = rms_norm(h, norm_ffn_w[l])
        u = jax.nn.relu(jnp.einsum('bsd,df->bsf', hn, w_ff1[l]))
        h = h + jnp.einsum('bsf,fd->bsd', u * u, w_ff2[l])
    return rms_norm(h, final_norm_w)


_drawn_inputs = setup_inputs


def setup_inputs(seed=0):
    import zlib

    import numpy as np

    out = dict(_drawn_inputs(seed))
    spreads = {}
    factors = {'norm_mix_w': 3.204,
     'conv_b': 36.667,
     'da_subln_w': 80.67,
     'ml_norm_w': 108.69,
     'norm_ffn_w': 12.223,
     'final_norm_w': 23.556}
    for name, (base, spread) in spreads.items():
        noise = np.random.default_rng([zlib.crc32(name.encode()), seed]).standard_normal(out[name].shape)
        drawn = base * np.exp(spread * noise) if base else spread * noise
        out[name] = __import__('jax').numpy.asarray(drawn.astype(out[name].dtype))
    for name, factor in factors.items():
        out[name] = (out[name] * factor).astype(out[name].dtype)
    return out
```

```python
from contextlib import ExitStack

import numpy as np

import concourse.bass as bass
from concourse import mybir

P = 128
F32 = mybir.dt.float32
F32R = mybir.dt.float32r
I32 = mybir.dt.int32
ALU = mybir.AluOpType
ACT = mybir.ActivationFunctionType
AX_X = mybir.AxisListType.X

D = 1024
S = 1024
KT = D // P
TT = S // P
HALF = S // 2
NH = 8
DK = 64
DV = 128
CONV = 4
DFF = 4 * D
EPS = 1e-6
LAMBDA_INIT = 0.2
SCALE = DK ** -0.5
NEG = -float(2 ** 100)
VW = DV + 2

OFF_Q, OFF_K, OFF_V = 0, 1024, 2048
OFF_MQ, OFF_MK, OFF_MV = 3072, 3584, 4096
OFF_I, OFF_F, OFF_O, OFF_G = 5120, 5128, 5136, 6160

HB = 6
N_GATE = NH * HB
N_PA = N_GATE + 16
N_PB = N_PA + KT
N_WO = N_PB + KT
N_FF = N_WO + KT
GROUPS = DFF // (KT * P)
N_ALL = N_FF + GROUPS * 2 * KT

X_RAW = 3
XB = 4

SLOTS = 16
UNIT_SLOTS = (0, 1, 2, 4, 5, 7, 8, 9, 10, 11, 12, 14)
UNITS_AT = [[k for k, at in enumerate(UNIT_SLOTS) if at == s] for s in range(SLOTS)]


def wait(eng, sem, value):
    if isinstance(value, int) and value <= 0:
        return
    eng.wait_ge(sem, value)


def tr_index(i, second):
    return i + max(0, i - 4) + (1 if second else 0)


def tr_last(i):
    return tr_index(i, i >= 4)


class Chain:

    def __init__(self, eng, sem, per_head):
        self.eng, self.sem, self.per_head = eng, sem, per_head
        self.base, self.count = 0, 0

    def start(self, base):
        self.base, self.count = base, 0

    def link(self, ins):
        self.count += 1
        ins.then_inc(self.sem, 1)
        self.eng.wait_ge(self.sem, self.base + self.count)


def build(nc, x, positions, norm_mix_w, w_in, ml_gate_b, conv_w, conv_b, da_lambda, da_subln_w,
          ml_norm_w, w_proj_a, w_proj_b, w_out, norm_ffn_w, w_ff1, w_ff2, final_norm_w,
          c_ident, c_inv, c_mask, c_last, c_carry, c_keep, out):
    x2 = x[0]
    out2 = out[0]
    w_in2, w_pa, w_pb, w_o, w_f1, w_f2 = w_in[0], w_proj_a[0], w_proj_b[0], w_out[0], w_ff1[0], w_ff2[0]

    proj_d = nc.dram_tensor("proj_d", (N_PA, P, S), F32, kind="Internal").ap()
    xT_d = nc.dram_tensor("xT_d", (KT, P, S), F32, kind="Internal").ap()
    oa_d = nc.dram_tensor("oa_d", (NH, P, S), F32, kind="Internal").ap()
    ob_d = nc.dram_tensor("ob_d", (NH, P, S), F32, kind="Internal").ap()
    u_d = nc.dram_tensor("u_d", (NH, S), F32, kind="Internal").ap()
    inter_d = nc.dram_tensor("inter_d", (NH, S), F32, kind="Internal").ap()

    with ExitStack() as ctx:
        def sb(name, shape, dt=F32, scope=ctx):
            return scope.enter_context(nc.sbuf_tensor(name, shape, dt))

        def ps(name, shape):
            return ctx.enter_context(nc.psum_tensor(name, shape, F32))

        def sem(name):
            return ctx.enter_context(nc.semaphore(name))

        raw = [sb(f"w_raw{i}", [P, KT, P]) for i in range(2)]
        wh = [sb(f"w_hi{i}", [P, KT, P], F32R) for i in range(2)]
        wl = [sb(f"w_lo{i}", [P, KT, P], F32R) for i in range(2)]
        r1h = sb("r1h", [P, KT, S], F32R)
        r1l = sb("r1l", [P, KT, S], F32R)
        ev = [sb(f"ev{i}", [P, HALF]) for i in range(2)]
        ident = sb("ident", [P, P])
        ones = sb("ones", [P, P])
        nw = sb("nw", [P, 2, KT])
        tk = sb("tk", [P, TT, 4, NH])
        dc = sb("dc", [P, TT, NH])
        cw = sb("cw", [P, CONV + 1, NH])
        mlw = sb("mlw", [P, NH])
        aw = sb("aw", [P, 1])
        neglam = sb("neglam", [P, 1])

        heads = ctx.enter_context(ExitStack())
        identr = sb("identr", [P, P], F32R, heads)
        keep = sb("keep", [P, P], F32, heads)
        mask = sb("mask", [P, 3 * P], F32R, heads)
        cosT = sb("cosT", [P, S], F32, heads)
        sinT = sb("sinT", [P, S], F32, heads)
        inv = sb("inv", [P, 1], F32, heads)
        ckq = sb("ckq", [P, CONV - 1 + S], F32, heads)
        kqs = sb("kqs", [P, S], F32, heads)
        sg = sb("sg", [P, S], F32, heads)
        qpad = sb("qpad", [P, S], F32, heads)
        v1 = sb("v1", [P, TT, VW], F32, heads)
        cst = sb("cst", [P, TT, VW], F32, heads)

        with ExitStack() as sc:
            xtok = [sb(f"xtok{i}", [P, D], F32, sc) for i in range(XB)]
            nwb = sb("nwb", [P, D], F32, sc)
            ss = sb("ss", [P, TT], F32, sc)
            rstd0 = sb("rstd0", [P, TT], F32, sc)
            xTs = [sb(f"xTs{i}", [P, KT, P], F32, sc) for i in range(2)]
            wif = sb("wif", [P, KT, 16], F32, sc)
            wifh = sb("wifh", [P, KT, P], F32R, sc)
            wifl = sb("wifl", [P, KT, P], F32R, sc)
            gb = sb("gb", [P, 1], F32, sc)
            lamt = sb("lamt", [P, 4 * DK], F32, sc)
            lams = sb("lams", [P, 4], F32, sc)
            irow = sb("irow", [NH, S], F32, sc)
            frow = sb("frow", [NH, S], F32, sc)
            erow = sb("erow", [NH, S], F32, sc)
            mrow = sb("mrow", [NH, S], F32, sc)
            brow = sb("brow", [NH, S], F32, sc)
            wrow = sb("wrow", [NH, S], F32, sc)
            mprev = sb("mprev", [NH, TT], F32, sc)
            carry = sb("carry", [NH, S], F32, sc)
            yrow = sb("yrow", [P, S], F32, sc)
            last = sb("last", [P, P], F32, sc)
        ga, urow = yrow, erow

        with heads, ExitStack() as sc:
            qraw = sb("qraw", [P, S], F32, sc)
            kraw = sb("kraw", [P, S], F32, sc)
            qs = sb("qs", [P, 2, S], F32R, sc)
            ka = sb("ka", [P, 2, S], F32R, sc)
            kb = sb("kb", [P, 2, S], F32R, sc)
            vs = sb("vs", [P, TT, 2 * DV], F32R, sc)
            pr = sb("pr", [P, 2, S], F32, sc)
            at = sb("at", [P, S], F32, sc)
            ath = sb("ath", [P, TT, P], F32R, sc)
            atl = sb("atl", [P, TT, P], F32R, sc)
            oo = sb("oo", [P, TT, DV], F32, sc)
            otmp = sb("otmp", [P, DV], F32, sc)
            sqj = sb("sqj", [P, DV], F32, sc)
            mx = sb("mx", [P, 2], F32, sc)
            nb = sb("nb", [P, 2], F32, sc)
            rs = sb("rs", [P, TT, 2], F32, sc)
            rr = sb("rr", [P, TT, 2], F32, sc)
            cc = sb("cc", [P, 1], F32, sc)
            sso = sb("sso", [P, TT], F32, sc)
            t8 = sb("t8", [P, TT], F32, sc)
            rsc = sb("rsc", [P, TT], F32, sc)
            nd = sb("nd", [P, TT, VW], F32, sc)
            osig = sb("osig", [P, S], F32, sc)
            hk = sb("hk", [P, TT, 4], F32, sc)
            hd = sb("hd", [P, TT], F32, sc)
            hc = sb("hc", [P, CONV + 1], F32, sc)
            hw = sb("hw", [P, 1], F32, sc)
            ssm = sb("ssm", [P, TT], F32, sc)
            d1 = sb("d1", [P, TT], F32, sc)
            d2 = sb("d2", [P, TT], F32, sc)
            rm = sb("rm", [P, TT], F32, sc)
        ckw = ckq[:, CONV - 1:].rearrange("p (c n) -> p c n", c=TT)
        ee = qraw

        with ExitStack() as sc:
            r2h = sb("r2h", [P, KT, S], F32R, sc)
            r2l = sb("r2l", [P, KT, S], F32R, sc)
            res = sb("res", [P, KT, S], F32, sc)
            with ExitStack() as s2:
                stg = [sb(f"stg{i}", [P, S], F32, s2) for i in range(2)]
                gt = [sb(f"gt{i}", [P, HALF], F32, s2) for i in range(2)]
            with ExitStack() as s2:
                sq1 = [sb(f"sq1{i}", [P, HALF], F32, s2) for i in range(2)]
                nt1 = [sb(f"nt1{i}", [P, HALF], F32, s2) for i in range(2)]
                rstd1 = sb("rstd1", [P, S], F32, s2)
            with ExitStack() as s2:
                ru = [sb(f"ru{i}", [P, HALF], F32, s2) for i in range(2)]
                ut = [sb(f"ut{i}", [P, HALF], F32, s2) for i in range(2)]
            with ExitStack() as s2:
                otok = [sb(f"otok{i}", [P, D], F32, s2) for i in range(2)]

        gp = [ps(f"gp{i}", [P, HALF]) for i in range(2)]
        sp_ = ps("scores", [P, 2, S])
        tr = ps("tr", [P, 512])
        ob = ps("ob", [P, 512])
        sbank = sp_[:, :, :].rearrange("p c (b n) -> p (c b) n", b=2)

        def nd_at(c):
            return sbank[:, c // 3, (c % 3) * VW:(c % 3 + 1) * VW]

        w_loaded = [sem(f"w_loaded{i}") for i in range(2)]
        w_loaded_q = sem("w_loaded_q")
        w_hi, w_split, gemm_done, gp_free = sem("w_hi_done"), sem("w_split"), sem("gemm_done"), sem("gp_free")
        ev_ready = [sem(f"ev_ready{i}") for i in range(2)]
        st = [sem(f"proj_stored{i}") for i in range(2)]
        ident_in, c2_in = sem("ident_in"), sem("head_consts_in")
        c_in, wif_in, nwb_in, x_in = sem("consts_in"), sem("wif_in"), sem("nwb_in"), [sem(f"x_in{i}") for i in range(XB)]
        ss_ready, x_var, x_std, x_rstd, x_scaled = (sem(n) for n in ("ss_ready", "x_var", "x_std", "x_rstd", "x_scaled"))
        x_tr, x_hi, x_lo = sem("x_transposed"), sem("x_hi"), sem("x_lo")
        xts_out, xt_st = sem("xts_out"), [sem("xt_stored0"), sem("xt_stored1")]
        sq_ready, sq_used, var_ready, std_ready = sem("sq_ready"), sem("sq_used"), sem("var_ready"), sem("std_ready")
        rstd_ready, nt_ready, n_hi, n_lo = sem("rstd_ready"), sem("nt_ready"), sem("n_hi"), sem("n_lo")
        ss_done = sem("sumsq_done")
        wif_set, wif_h, wif_l, if_done = sem("wif_set"), sem("wif_h"), sem("wif_l"), sem("if_done")
        pdv, pact, ppl = sem("prologue_dve"), sem("prologue_act"), sem("prologue_pool")
        nf_ready, ln_ready, rows_ready, wrow_ready, tk_tr, tk_ready, dc_done, tk_done = (
            sem("nf_ready"), sem("ln_ready"), sem("rows_ready"), sem("wrow_ready"), sem("tk_tr"), sem("tk_ready"),
            sem("dc_done"), sem("tk_done"))
        uw_st = sem("uw_stored")
        ang_ready, tab_ready, lam_ready, lam_exp = sem("ang_ready"), sem("tab_ready"), sem("lam_ready"), sem("lam_exp")
        init_done = sem("init_done")
        q_in, k_in, v_in, kq_in, mv_in, o_in, u_in, i_in = (sem(n) for n in (
            "q_in", "k_in", "v_in", "kq_in", "mv_in", "o_in", "u_in", "inter_in"))
        roped, qk_hi, qk_lo, kb_in = sem("roped"), sem("qk_hi"), sem("qk_lo"), sem("kb_in")
        vtr, v_hi, v_lo, mv_out = sem("vtr"), sem("v_hi"), sem("v_lo"), sem("mv_out")
        s_done, nb_ready, exp_done, a_done = sem("s_done"), sem("nb_ready"), sem("exp_done"), sem("a_done")
        tr_done, a_hi, a_lo, pv_done = sem("tr_done"), sem("a_hi"), sem("a_lo"), sem("pv_done")
        o_right, o_add, sso_done, varo, stdo, osc = (sem(n) for n in ("o_right", "o_add", "sso_done", "varo", "stdo", "osc"))
        ot_tr, ot_out, oa_st = sem("ot_tr"), sem("ot_out"), sem("oa_stored")
        hk_ready, conv_done, sg_ready, os_ready, kq_ready, qp_ready = (sem(n) for n in (
            "hk_ready", "conv_done", "sg_ready", "os_ready", "kq_ready", "qp_ready"))
        e_exp, e_sel, st_done, kt_done, pt_done, kw_done, kv_done, c_done, qi_ready = (sem(n) for n in (
            "e_exp", "e_sel", "st_done", "kt_done", "pt_done", "kw_done", "kv_done", "c_done", "qi_ready"))
        nd_done, nd_out, ssm_done, varm, stdm, hm_ready, hm_tr, obt, ob_st = (sem(n) for n in (
            "nd_done", "nd_out", "ssm_done", "varm", "stdm", "hm_ready", "hm_tr", "obt", "ob_stored"))
        dve_chain = sem("dve_chain")
        stg_in, stg_hi, stg_lo = [sem("stg_in0"), sem("stg_in1")], sem("stg_hi"), sem("stg_lo")
        g_in, g_sig, g_used = [sem("g_in0"), sem("g_in1")], sem("g_sig"), sem("g_used")
        m_sum, m_ready, m_hi, m_lo, res_in = sem("m_sum"), sem("m_ready"), sem("m_hi"), sem("m_lo"), sem("res_in")
        res_done = sem("res_done")
        r_ready, u_ready, u_hi, u_lo, ff_done = sem("r_ready"), sem("u_ready"), sem("u_hi"), sem("u_lo"), sem("ff_done")
        fin_ready, ft_tr, ft_out, out_st = sem("fin_ready"), sem("ft_tr"), sem("ft_out"), [sem("out_st0"), sem("out_st1")]

        DVE_HEAD = 46

        def col_block(w, first):
            return w.rearrange("(k p) n -> p k n", p=P)[:, :, bass.ds(first, P)]

        block = ctx.enter_context(nc.Block())

        @block.sync
        def _(sp):
            def wload(n, half_n, slot, src):
                wait(sp, w_split, n - 1)
                sp.dma_start(raw[slot][:], src).then_inc(w_loaded[slot], 16)

            def wload_head(h, b):
                n = h * HB + b
                if b == 3:
                    wait(sp, w_split, n - 1)
                    for j, off in enumerate((OFF_MK, OFF_MQ)):
                        src = w_in2.rearrange("(k p) n -> p k n", p=P)[:, :, bass.ds(h * DK + off, DK)]
                        sp.dma_start(raw[1][:, :, j * DK:(j + 1) * DK], src).then_inc(
                            (w_loaded[1], w_loaded_q)[j], 16)
                else:
                    off = (OFF_Q, OFF_K, OFF_V, None, OFF_MV, OFF_O)[b]
                    wload(n, None, b % 2, col_block(w_in2, h * P + off))

            def store(n, base, b):
                for i in range(2):
                    sp.wait_ge(ev_ready[i], n + 1)
                    sp.dma_start(proj_d[bass.ds(n, 1), :, i * HALF:(i + 1) * HALF].rearrange("a p n -> (a p) n"),
                                 ev[i][:]).then_inc(st[i], 16)

            def head_src(h, b):
                return proj_d[bass.ds(h * HB + b, 1)].rearrange("a p n -> (a p) n")

            def turned_rows(to, src, s_in):
                for c in range(2):
                    for half in range(2):
                        a, b = c * DK + half * 8, c * DK + (1 - half) * 8
                        sp.dma_start(to[a:a + 8, :], src[b:b + 8, :]).then_inc(s_in, 16)

            def att_loads(h):
                if isinstance(h, int) and h == 0:
                    sp.wait_ge(init_done, 3)
                for i in range(2):
                    sp.wait_ge(st[i], 16 * (h * HB + HB))
                wait(sp, qi_ready, h)
                sp.dma_start(kraw[:], head_src(h, 1)).then_inc(k_in, 16)
                wait(sp, kt_done, h)
                turned_rows(kqs, head_src(h, 1), k_in)
                wait(sp, nd_done, h)
                sp.dma_start(qraw[:], head_src(h, 0)).then_inc(q_in, 16)
                wait(sp, kq_ready, h)
                turned_rows(sg, head_src(h, 0), q_in)
                wait(sp, a_done, NH * h)
                sp.dma_start(pr[:, 0, :], head_src(h, 2)).then_inc(v_in, 16)
                sp.dma_start(pr[:, 1, :], head_src(h, 4)).then_inc(mv_in, 16)
                wait(sp, kv_done, h)
                sp.dma_start(ckq[:, CONV - 1:], head_src(h, 3)).then_inc(kq_in, 16)
                wait(sp, ob_st, 16 * h)
                sp.dma_start(osig[:], head_src(h, 5)).then_inc(o_in, 16)

            def row_loads(h):
                sp.wait_ge(qk_lo, 4 * h + 4)
                if isinstance(h, int) and h == 0:
                    sp.wait_ge(uw_st, 32)
                for buf, src, s_in in ((qraw, u_d, u_in), (kraw, inter_d, i_in)):
                    row = src[bass.ds(h, 1), :].rearrange("a n -> (a n)").partition_broadcast(P)
                    sp.dma_start(buf[:], row).then_inc(s_in, 16)

            def x_load(j):
                wait(sp, x_tr, 2 * (j - XB + 1))
                t = j % TT
                sp.dma_start(xtok[j % XB][:], x2[t * P:(t + 1) * P, :]).then_inc(x_in[j % XB], 16)

            def x_store(t):
                sp.wait_ge(xts_out, 2 * t + 2)
                sp.dma_start(xT_d[:, :, t * P:(t + 1) * P].rearrange("k p n -> p k n"), xTs[t % 2][:]).then_inc(xt_st[t % 2], 16)

            for j in range(TT + XB):
                x_load(j)
                if j == 0:
                    sp.dma_start(nwb[:], norm_mix_w[0].partition_broadcast(P)).then_inc(nwb_in, 16)
                    sp.dma_start(ident[:], c_ident).then_inc(ident_in, 16)
                if j == 3:
                    wload_head(0, 0)
                if j == 6:
                    wload_head(0, 1)
            def head_round(h, att, first=False):
                for b in range(HB):
                    if not (first and b < 2):
                        wload_head(h, b)
                    if isinstance(h, int):
                        for t in (2 * (h * HB + b) - 7, 2 * (h * HB + b) - 6):
                            if 0 <= t < TT:
                                if t + XB < TT:
                                    x_load(TT + XB + t)
                                x_store(t)
                    if isinstance(h, int) and h == 1 and b == 0:
                        sp.wait_ge(rows_ready, 1)
                        sp.dma_start(u_d, urow[:]).then_inc(uw_st, 16)
                        sp.wait_ge(wrow_ready, 1)
                        sp.dma_start(inter_d, wrow[:]).then_inc(uw_st, 16)
                    if b >= 2:
                        store(h * HB + b - 2, None, b)
                    elif not first:
                        store(h * HB + b - 2, None, b)
                    if att is not None and b == 1:
                        att_loads(att)
                    if att is not None and b == 2:
                        row_loads(att)

            head_round(0, None, first=True)
            head_round(1, 0)
            with sp.Fori(2, NH) as h:
                head_round(h, h - 1)
            for j in range(16):
                n = N_GATE + j
                wload(n, None, n % 2, col_block(w_in2, OFF_G + j * P))
                store(n - 2, None, None)
                if j == 1:
                    att_loads(NH - 1)
                if j == 2:
                    row_loads(NH - 1)
            for k in range(2):
                wload(N_PA + k, None, k, col_block(w_pa, k * P))
                store(N_PA - 2 + k, None, None)
            for i in range(2):
                sp.wait_ge(st[i], 16 * N_PA)
            sp.wait_ge(oa_st, 16 * NH)
            sp.wait_ge(ob_st, 16 * NH)

            def stage_in(k, src):
                wait(sp, stg_lo, k - 1)
                sp.dma_start(stg[k % 2][:], src).then_inc(stg_in[k % 2], 16)

            def gate_in(j):
                for i in range(2):
                    wait(sp, g_used, 2 * (j - 1) + i + 1 if j else 0)
                    sp.dma_start(gt[i][:], proj_d[N_GATE + j, :, i * HALF:(i + 1) * HALF]).then_inc(g_in[i], 16)

            for k in range(KT):
                stage_in(k, oa_d[k])
            for j in range(2 * KT):
                n = N_PA + j + 2
                if n < N_PB:
                    src = col_block(w_pa, (n - N_PA) * P)
                elif n < N_WO:
                    src = col_block(w_pb, (n - N_PB) * P)
                else:
                    src = col_block(w_o, (n - N_WO) * P)
                gate_in(j)
                wload(n, None, n % 2, src)
                if j < KT:
                    stage_in(KT + j, ob_d[j])
                else:
                    k = j - KT
                    sp.wait_ge(m_sum, 2 * k + 2)
                    sp.dma_start(res[:, k, :], xT_d[k]).then_inc(res_in, 16)
            for k in range(KT):
                n = N_WO + k + 2
                src = col_block(w_o, (n - N_WO) * P) if n < N_FF else col_block(w_f1, (n - N_FF) * P)
                wload(n, None, n % 2, src)

            def ff_loads(g, last):
                n0 = 2 * KT * g + N_FF
                for b in range(2, 2 * KT + 2):
                    if b < KT:
                        src = col_block(w_f1, g * (KT * P) + b * P)
                    elif b < 2 * KT:
                        src = w_f2.rearrange("(g k p) n -> g p k n", p=P, k=KT)[
                            bass.ds(g, 1), :, :, (b - KT) * P:(b - KT + 1) * P].rearrange("a p k n -> (a p) k n")
                    elif last:
                        break
                    else:
                        src = col_block(w_f1, (g + 1) * (KT * P) + (b - 2 * KT) * P)
                    wload(n0 + b, None, b % 2, src)

            with sp.Fori(0, GROUPS - 1) as g:
                ff_loads(g, False)
            ff_loads(GROUPS - 1, True)
            for t in range(TT):
                sp.wait_ge(ft_out, 2 * t + 2)
                sp.dma_start(out2[t * P:(t + 1) * P, :], otok[t % 2][:]).then_inc(out_st[t % 2], 16)
            for i in range(2):
                sp.wait_ge(out_st[i], 16 * (TT // 2))
            for i in range(2):
                sp.wait_ge(xt_st[i], 16 * (TT // 2))

        @block.tensor
        def _(pe):
            def unit(n, slot, half, mh, ml, before_k=None):
                if half == 0:
                    pe.wait_ge(w_split, n + 1)
                wait(pe, gp_free, 2 * n + half - 1)
                t = slice(half * HALF, (half + 1) * HALF)
                for k in range(KT):
                    if before_k:
                        before_k(k)
                    pe.matmul(gp[half][:], wh[slot][:, k, :], mh[:, k, t], start=(k == 0), stop=False)
                    pe.matmul(gp[half][:], wh[slot][:, k, :], ml[:, k, t], start=False, stop=False)
                    mm = pe.matmul(gp[half][:], wl[slot][:, k, :], mh[:, k, t], start=False, stop=(k == KT - 1))
                mm.then_inc(gemm_done, 1)

            def sum_squares(stage, sq, tiles=range(KT)):
                for k in tiles:
                    for i in range(2):
                        m = 2 * KT * stage + 2 * k + i
                        pe.wait_ge(sq_ready, m + 1)
                        mm = pe.matmul(sbank[:, i, :], ones[:], sq[i][:], start=(k == 0), stop=(k == KT - 1))
                        mm.then_inc(sq_used, 1)

            def x_transpose(j):
                if j < TT:
                    pe.wait_ge(x_scaled, j + 1)
                else:
                    pe.wait_ge(x_in[j % XB], 16 * (j // XB + 1))
                for i in range(2):
                    if j <= TT:
                        wait(pe, x_lo, 2 * (j - 1) + i + 1 if j else 0)
                    else:
                        pe.wait_ge(xts_out, 2 * (j - TT - 1) + i + 1)
                    for n in range(4):
                        k = 4 * i + n
                        mm = pe.transpose([tr, ob][i][:, n * P:(n + 1) * P], xtok[j % XB][:, k * P:(k + 1) * P], ident[:])
                    mm.then_inc(x_tr, 1)

            def gates_half(i, tiles):
                t = slice(i * HALF, (i + 1) * HALF)
                for k in range(KT):
                    if k in tiles:
                        x_transpose(tiles[k])
                    if k == 0:
                        pe.wait_ge(x_lo, TT * (i + 1))
                        pe.wait_ge(wif_l, 1)
                    pe.matmul(sbank[:, i, :], wifh[:, k, :], r1h[:, k, t], start=(k == 0), stop=False)
                    pe.matmul(sbank[:, i, :], wifh[:, k, :], r1l[:, k, t], start=False, stop=False)
                    mm = pe.matmul(sbank[:, i, :], wifl[:, k, :], r1h[:, k, t], start=False, stop=(k == KT - 1))
                mm.then_inc(if_done, 1)

            pe.wait_ge(ident_in, 16)
            for j in range(4):
                x_transpose(j)
            gates_half(0, {2: 4, 6: 5})
            unit(0, 0, 0, r1h, r1l, before_k=lambda k: x_transpose(6 + k // 4) if k in (2, 6) else None)
            gates_half(1, {})

            def head_unit(h, k):
                b = k // 2
                unit(h * HB + b, b % 2, k % 2, r1h, r1l)

            for k in range(2 * HB):
                if k:
                    head_unit(0, k)
                if X_RAW <= k < X_RAW + TT:
                    x_transpose(TT + k - X_RAW)
                if k == 7:
                    pe.wait_ge(rows_ready, 1)
                    for c in range(TT):
                        mm = pe.transpose(sbank[:, c // 4, (c % 4) * P:(c % 4 + 1) * P], yrow[:, c * P:(c + 1) * P], ident[:])
                    mm.then_inc(tk_tr, 1)
                if k == 9:
                    pe.wait_ge(tk_ready, 1)
                    pe.matmul(sbank[:, 2, 0:TT * NH], last[:], tk[:, :, 1, :], start=True, stop=True).then_inc(dc_done, 1)

            def attend(h, s):
                if s == 0 and isinstance(h, int) and h == 0:
                    pe.wait_ge(tk_done, 1)
                    pe.wait_ge(init_done, 3)
                if s in (0, 2):
                    c = s // 2
                    pe.wait_ge((v_in, mv_in)[c], 16 * h + 16)
                    if c == 0:
                        wait(pe, obt, 2 * h)
                    else:
                        pe.wait_ge(v_lo, 2 * h + 2)
                    for i, bank in enumerate((tr, ob)):
                        for j in range(4):
                            t = 4 * i + j
                            mm = pe.transpose(bank[:, j * P:(j + 1) * P], pr[:, c, t * P:(t + 1) * P], ident[:])
                        mm.then_inc(vtr, 1)
                i = s - 5
                if 0 <= i < TT:
                    pe.wait_ge(a_lo, 12 * h + tr_last(i) + 1)
                    if i == 0:
                        pe.wait_ge(mv_out, 2 * h + 2)
                    else:
                        pe.wait_ge(o_add, TT * h + i)
                    for j in range(i + 1):
                        pe.matmul(ob[:, 0:2 * DV], ath[:, j, :], vs[:, j, :], start=(j == 0), stop=False)
                        mm = pe.matmul(ob[:, 0:2 * DV], atl[:, j, :], vs[:, j, :], start=False, stop=(j == i))
                    mm.then_inc(pv_done, 1)
                i = s - 4
                if 0 <= i < TT:
                    pe.wait_ge(a_done, TT * h + i + 1)
                    if i == 0:
                        pe.wait_ge(mv_out, 2 * h + 2)
                    else:
                        pe.wait_ge(a_lo, 12 * h + tr_index(i, False))
                    for j in range(min(4, i + 1)):
                        mm = pe.transpose(tr[:, j * P:(j + 1) * P], at[:, j * P:(j + 1) * P], ident[:])
                    mm.then_inc(tr_done, 1)
                i = s - 3
                if 0 <= i < TT:
                    if i == 0:
                        pe.wait_ge(qk_lo, 4 * h + 4)
                        pe.wait_ge(kb_in, 32 * h + 32)
                        wait(pe, nd_out, 3 * h)
                    else:
                        pe.wait_ge(exp_done, 2 * (TT * h + i))
                    width = -(-(i + 1) // 2) * 2 * P
                    edges = [(0, width)] if width <= 512 else [(0, 512), (512, width)]
                    m0 = width - 2 * P
                    moff = 0 if i % 2 else P
                    for c in range(2):
                        for lo, hi in edges:
                            diag = lo <= m0 < hi
                            q = qs[:, c, i * P:(i + 1) * P]
                            if diag:
                                pe.matmul(sp_[:, c, m0:m0 + 2 * P], identr[:], mask[:, moff:moff + 2 * P],
                                          start=True, stop=False, skip_group_check=True)
                            pe.matmul(sp_[:, c, lo:hi], q, ka[:, c, lo:hi], start=not diag, stop=False,
                                      skip_group_check=True)
                            mm = pe.matmul(sp_[:, c, lo:hi], q, kb[:, c, lo:hi], start=False, stop=True,
                                           skip_group_check=True)
                        mm.then_inc(s_done, 1)
                i = s - 4
                if 4 <= i < TT:
                    pe.wait_ge(a_lo, 12 * h + tr_index(i, True))
                    for j in range(4, i + 1):
                        mm = pe.transpose(tr[:, (j - 4) * P:(j - 3) * P], at[:, j * P:(j + 1) * P], ident[:])
                    mm.then_inc(tr_done, 1)
                if s == 11:
                    pe.wait_ge(kq_ready, h + 1)
                    pe.wait_ge(qp_ready, h + 1)
                    pe.wait_ge(exp_done, 2 * TT * (h + 1))
                    for c in range(TT):
                        ch = slice(c * P, (c + 1) * P)
                        mm = pe.matmul(sp_[:, 0, ch], kqs[:, ch], qpad[:, ch], start=True, stop=True)
                    mm.then_inc(st_done, 1)
                    for c in range(TT):
                        ch = slice(c * P, (c + 1) * P)
                        mm = pe.transpose(sp_[:, 1, ch], kqs[:, ch], ident[:])
                    mm.then_inc(kt_done, 1)
                if s == 12:
                    pe.wait_ge(kw_done, 2 * h + 2)
                    pe.wait_ge(pt_done, 2 * h + 2)
                    for c in range(TT - 1):
                        mm = pe.matmul(nd_at(c), ckw[:, c, :], v1[:, c, :], start=True, stop=True)
                    mm.then_inc(kv_done, 1)
                if s == 13:
                    pe.wait_ge(c_done, h + 1)
                    pe.wait_ge(qi_ready, h + 1)
                    for c in range(TT):
                        ch = slice(c * P, (c + 1) * P)
                        mm = pe.matmul(nd_at(c), ee[:, ch], v1[:, c, :], start=True, stop=(c == 0))
                        if c:
                            mm = pe.matmul(nd_at(c), qpad[:, ch], cst[:, c, :], start=False, stop=True)
                    mm.then_inc(nd_done, 1)
                    pe.wait_ge(osc, h + 1)
                    for i, bank in enumerate((tr, ob)):
                        for j in range(4):
                            mm = pe.transpose(bank[:, j * P:(j + 1) * P], oo[:, 4 * i + j, :], ident[:])
                        mm.then_inc(ot_tr, 1)
                if s == 15:
                    pe.wait_ge(hm_ready, h + 1)
                    pe.wait_ge(ot_out, 2 * h + 2)
                    for i, bank in enumerate((tr, ob)):
                        for j in range(4):
                            mm = pe.transpose(bank[:, j * P:(j + 1) * P], nd[:, 4 * i + j, 0:DV], ident[:])
                        mm.then_inc(hm_tr, 1)

            def head_round(h, att):
                for s in range(SLOTS):
                    for k in UNITS_AT[s]:
                        head_unit(h, k)
                    attend(att, s)

            head_round(1, 0)
            with pe.Fori(2, NH) as h:
                head_round(h, h - 1)
            for s in range(SLOTS):
                for i in range(2):
                    unit(N_GATE + s, s % 2, i, r1h, r1l)
                attend(NH - 1, s)

            for b in range(KT):
                for i in range(2):
                    unit(N_PA + b, b % 2, i, r2h, r2l, before_k=(lambda k: pe.wait_ge(stg_lo, k + 1)) if b + i == 0 else None)
            for b in range(KT):
                for i in range(2):
                    if b + i == 0:
                        pe.wait_ge(stg_lo, 2 * KT)
                    unit(N_PB + b, b % 2, i, r1h, r1l)
            for b in range(KT):
                for i in range(2):
                    unit(N_WO + b, b % 2, i, r2h, r2l,
                         before_k=(lambda k, i=i: pe.wait_ge(m_lo, 2 * k + i + 1)) if b == 0 else None)
                if b:
                    sum_squares(0, sq1, [b - 1])
            sum_squares(0, sq1, [KT - 1])

            def ff_group(g, first=False):
                n0 = g * (2 * KT) + N_FF
                for b in range(KT):
                    for i in range(2):
                        unit(n0 + b, b % 2, i, r1h, r1l,
                             before_k=(lambda k, i=i: pe.wait_ge(n_lo, 2 * k + i + 1)) if first and b == 0 else None)
                for b in range(KT):
                    for i in range(2):
                        unit(n0 + KT + b, b % 2, i, r2h, r2l,
                             before_k=(lambda k, i=i: pe.wait_ge(u_lo, g * (2 * KT) + 2 * k + i + 1)) if b == 0 else None)

            ff_group(0, first=True)
            with pe.Fori(1, GROUPS) as g:
                ff_group(g)
            sum_squares(1, sq1)
            for t in range(TT):
                for i in range(2):
                    if t >= 2:
                        pe.wait_ge(ft_out, 2 * (t - 2) + i + 1)
                    for j in range(4):
                        k = 4 * i + j
                        if t == 0:
                            pe.wait_ge(fin_ready, 2 * k + 2)
                        mm = pe.transpose(sbank[:, 2 * (t % 2) + i, j * P:(j + 1) * P], res[:, k, t * P:(t + 1) * P], ident[:])
                    mm.then_inc(ft_tr, 1)

        @block.scalar
        def _(act):
            def split_hi(n, half_n, slot):
                act.wait_ge(w_loaded[slot], 16 * half_n + 16)
                wait(act, gemm_done, 2 * n - 2)
                act.activation(wh[slot][:], raw[slot][:], ACT.Copy).then_inc(w_hi, 1)

            def evac(n, half):
                wait(act, st[half], 16 * n)
                act.wait_ge(gemm_done, 2 * n + half + 1)
                act.activation(ev[half][:], gp[half][:], ACT.Copy).then_inc(gp_free, 1)
                act.wait_ge(gp_free, 2 * n + half + 1)
                act.sem_inc(ev_ready[half], 1)

            act.dma_start(wif[:], w_in2.rearrange("(k p) n -> p k n", p=P)[:, :, OFF_I:OFF_I + 16], allow_slow_non_contiguous=True).then_inc(wif_in, 16)
            act.dma_start(gb[0:NH, :], ml_gate_b[0, 0:NH].rearrange("(p a) -> p a", a=1), allow_slow_non_contiguous=True).then_inc(c_in, 16)
            act.dma_start(gb[32:32 + NH, :], ml_gate_b[0, NH:2 * NH].rearrange("(p a) -> p a", a=1), allow_slow_non_contiguous=True).then_inc(c_in, 16)
            act.dma_start(lamt[:], da_lambda[0].rearrange("a b -> (a b)").partition_broadcast(P), allow_slow_non_contiguous=True).then_inc(c_in, 16)
            act.dma_start(carry[:], c_carry, allow_slow_non_contiguous=True).then_inc(c_in, 16)
            act.dma_start(last[:], c_last, allow_slow_non_contiguous=True).then_inc(c_in, 16)

            def squares(stage, src, sq):
                for k in range(KT):
                    for i in range(2):
                        m = 2 * KT * stage + 2 * k + i
                        wait(act, sq_used, m - 1 if m % (2 * KT) >= 2 else 0)
                        act.activation(sq[i][:], src[:, k, i * HALF:(i + 1) * HALF], ACT.Square).then_inc(sq_ready, 1)

            def norm_root(stage, rstd):
                for i in range(2):
                    act.wait_ge(var_ready, 2 * stage + i + 1)
                    r = rstd[:, i * HALF:(i + 1) * HALF]
                    act.activation(r, r, ACT.Sqrt).then_inc(std_ready, 1)

            def norm_hi(stage, nt, k_of):
                for k in range(KT):
                    for i in range(2):
                        act.wait_ge(nt_ready, 2 * KT * stage + 2 * k + i + 1)
                        act.activation(r1h[:, k, i * HALF:(i + 1) * HALF], nt[i][:], ACT.Copy).then_inc(n_hi, 1)

            for t in range(TT + 2):
                if t < TT:
                    act.wait_ge(x_in[t % XB], 16 * (t // XB + 1))
                    wait(act, ss_ready, t)
                    act.activation(sp_[:, 1, :], xtok[t % XB][:], ACT.Square, accum_out=ss[:, t:t + 1]).then_inc(ss_ready, 1)
                if 1 <= t <= TT:
                    act.wait_ge(x_var, t)
                    act.activation(rstd0[:, t - 1:t], rstd0[:, t - 1:t], ACT.Sqrt).then_inc(x_std, 1)
                if t >= 2:
                    for i in range(2):
                        act.wait_ge(x_tr, 2 * (t - 2) + i + 1)
                        act.activation(r1h[:, 4 * i:4 * i + 4, (t - 2) * P:(t - 1) * P],
                                       (tr, ob)[i][:].rearrange("p (k n) -> p k n", k=4), ACT.Copy).then_inc(x_hi, 1)
                if t == 3:
                    act.wait_ge(wif_in, 16)
                    act.wait_ge(wif_set, 2)
                    act.activation(wifh[:, :, 0:NH], wif[:, :, 0:NH], ACT.Copy).then_inc(wif_h, 1)
                    act.activation(wifh[:, :, 32:32 + NH], wif[:, :, NH:2 * NH], ACT.Copy).then_inc(wif_h, 1)
                if t == 6:
                    split_hi(0, 0, 0)
            act.dma_start(nw[:, 0, :], norm_ffn_w[0].rearrange("(k p) -> p k", p=P), allow_slow_non_contiguous=True).then_inc(c_in, 16)
            act.dma_start(nw[:, 1, :], final_norm_w.rearrange("(k p) -> p k", p=P), allow_slow_non_contiguous=True).then_inc(c_in, 16)
            act.dma_start(aw[:], da_subln_w[0].rearrange("(p a) -> p a", a=1), allow_slow_non_contiguous=True).then_inc(c_in, 16)
            act.dma_start(mlw[:], ml_norm_w[0].rearrange("(h p) -> p h", p=P), allow_slow_non_contiguous=True).then_inc(c_in, 16)
            for j in range(CONV + 1):
                src = conv_w[0, j] if j < CONV else conv_b[0]
                act.dma_start(cw[0:DK, j, :], src[NH * DK:].rearrange("(h p) -> p h", p=DK), allow_slow_non_contiguous=True).then_inc(c_in, 16)
                act.dma_start(cw[DK:P, j, :], src[0:NH * DK].rearrange("(h p) -> p h", p=DK), allow_slow_non_contiguous=True).then_inc(c_in, 16)

            def xt_evac(t):
                wait(act, xt_st[t % 2], 16 * (t // 2))
                for i in range(2):
                    act.wait_ge(x_tr, 2 * (TT + t) + i + 1)
                    act.activation(xTs[t % 2][:, 4 * i:4 * i + 4, :], (tr, ob)[i][:].rearrange("p (k n) -> p k n", k=4),
                                   ACT.Copy).then_inc(xts_out, 1)

            def prologue_step(k):
                if k == 2:
                    for i, tab in enumerate((sinT, cosT)):
                        act.wait_ge(ang_ready, i + 1)
                        act.activation(tab[:], tab[:], ACT.Sin).then_inc(tab_ready, 1)
                if k == 4:
                    act.wait_ge(nf_ready, 1)
                    act.activation(erow[:], erow[:], ACT.Exp).then_inc(pact, 1)
                    act.wait_ge(pact, 1)
                    act.activation(erow[:], erow[:], ACT.Ln, bias=1.0).then_inc(ln_ready, 1)
                    act.wait_ge(lam_ready, 1)
                    act.activation(lams[:, 2:4], lams[:, 0:2], ACT.Exp).then_inc(lam_exp, 1)
                if k == 6:
                    act.wait_ge(rows_ready, 1)
                    act.activation(wrow[:], yrow[32:32 + NH, :], ACT.Exp).then_inc(wrow_ready, 1)
                if k == 8:
                    act.wait_ge(tk_tr, 1)
                    src = sbank[:, 0:2, :].rearrange("p b (c q r) -> p (b c) q r", c=4, q=4)[:, :, :, 0:NH]
                    for q in range(4):
                        act.activation(tk[:, :, q, :], src[:, :, q, :], ACT.Copy if q == 0 else ACT.Exp).then_inc(
                            tk_ready if q == 3 else pact, 1)
                if k == 10:
                    act.wait_ge(dc_done, 1)
                    act.activation(dc[:], sbank[:, 2, 0:TT * NH].rearrange("p (c h) -> p c h", c=TT), ACT.Copy).then_inc(tk_done, 1)
                    act.wait_ge(tk_done, 1)

            def units_of_round(h, k):
                if k % 2 == 0:
                    b = k // 2
                    split_hi(h * HB + b + 1, h * (HB // 2) + (b + 1) // 2, (b + 1) % 2)
                    
            def kq_wait(h, b):
                if b + 1 == 3:
                    act.wait_ge(w_loaded_q, 16 * h + 16)

            for k in range(2 * HB):
                kq_wait(0, k // 2)
                units_of_round(0, k)
                evac(k // 2, k % 2)
                prologue_step(k)
                if X_RAW <= k < X_RAW + TT:
                    xt_evac(k - X_RAW)

            def attend(h, s):
                def v_part(i):
                    act.wait_ge(vtr, 4 * h + 1 + i)
                    src = (tr, ob)[i][:].rearrange("p (t n) -> p t n", t=4)
                    act.activation(vs[:, 4 * i:4 * i + 4, 0:DV], src, ACT.Copy).then_inc(v_hi, 1)

                if s == 0:
                    v_part(0)
                    v_part(1)
                if s == 1:
                    for c, (x_, to) in enumerate(((kraw, ka), (qraw, qs))):
                        act.wait_ge(roped, 2 * h + c + 1)
                        act.activation(to[0:DK, 0, :], x_[0:DK, :], ACT.Copy).then_inc(qk_hi, 1)
                        act.activation(to[DK:P, 1, :], x_[DK:P, :], ACT.Copy).then_inc(qk_hi, 1)
                    act.wait_ge(qk_lo, 4 * h + 2)
                    act.dma_start(kb[0:DK, :, :].bitcast(F32), ka[DK:P, :, :].bitcast(F32)).then_inc(kb_in, 16)
                    act.dma_start(kb[DK:P, :, :].bitcast(F32), ka[0:DK, :, :].bitcast(F32)).then_inc(kb_in, 16)
                if s == 2:
                    for i in range(2):
                        act.wait_ge(vtr, 4 * h + 3 + i)
                        src = (tr, ob)[i][:].rearrange("p (t n) -> p t n", t=4)
                        act.activation(v1[:, 4 * i:4 * i + 4, 0:DV], src, ACT.Copy).then_inc(mv_out, 1)
                i = s - 5
                if 0 <= i < TT:
                    act.wait_ge(pv_done, TT * h + i + 1)
                    wait(act, sso_done, TT * h + i)
                    act.activation(otmp[:], ob[:, DV:2 * DV], ACT.Copy).then_inc(o_right, 1)

                def high(i, second):
                    act.wait_ge(tr_done, 12 * h + tr_index(i, second) + 1)
                    if not second:
                        wait(act, pv_done, TT * h + i)
                    j0, j1 = (4, i + 1) if second else (0, min(4, i + 1))
                    act.activation(ath[:, j0:j1, :], tr[:, 0:(j1 - j0) * P].rearrange("p (j n) -> p j n", n=P),
                                   ACT.Copy).then_inc(a_hi, 1)

                i = s - 4
                if 0 <= i < TT:
                    high(i, False)
                    if i >= 4:
                        high(i, True)
                i = s - 5
                if 0 <= i < TT:
                    act.wait_ge(o_add, TT * h + i + 1)
                    act.activation(otmp[:], oo[:, i, :], ACT.Square, accum_out=sso[:, i:i + 1]).then_inc(sso_done, 1)
                i = s - 3
                if 0 <= i < TT:
                    act.wait_ge(nb_ready, TT * h + i + 1)
                    wait(act, a_done, TT * h + i)
                    for c in range(2):
                        act.activation(pr[:, c, 0:(i + 1) * P], sp_[:, c, 0:(i + 1) * P], ACT.Exp, bias=nb[:, c:c + 1],
                                       scale=SCALE, accum_out=rs[:, i, c:c + 1]).then_inc(exp_done, 1)
                if s in (4, 5):
                    if s == 4:
                        act.wait_ge(u_in, 16 * h + 16)
                        act.wait_ge(hk_ready, 4 * h + 4)
                    for c in range(4 * (s - 4), 4 * (s - 4) + 4):
                        ch = slice(c * P, (c + 1) * P)
                        act.activation(ee[:, ch], ee[:, ch], ACT.Exp, bias=hk[:, c, 0:1]).then_inc(e_exp, 1)
                if s == 7:
                    act.wait_ge(conv_done, h + 1)
                    act.activation(sg[:], kqs[:], ACT.Sigmoid).then_inc(sg_ready, 1)
                    act.wait_ge(o_in, 16 * h + 16)
                    act.activation(osig[:], osig[:], ACT.Sigmoid).then_inc(os_ready, 1)
                if s == 9:
                    act.wait_ge(kq_ready, h + 1)
                    act.activation(qpad[0:DK, :], kqs[DK:P, :], ACT.Copy, scale=SCALE).then_inc(qp_ready, 1)
                if s == 12:
                    act.wait_ge(varo, h + 1)
                    act.activation(t8[:], t8[:], ACT.Sqrt).then_inc(stdo, 1)
                if s == 13:
                    act.wait_ge(nd_done, h + 1)
                    for b in range(3):
                        n = min(3, TT - 3 * b)
                        act.activation(nd[:, 3 * b:3 * b + n, :], sbank[:, b, 0:n * VW].rearrange("p (c n) -> p c n", n=VW),
                                       ACT.Copy).then_inc(nd_out, 1)
                    for i in range(2):
                        act.wait_ge(ot_tr, 2 * h + i + 1)
                        act.activation(at[:, i * HALF:(i + 1) * HALF], (tr, ob)[i][:], ACT.Copy, scale=aw[:, 0:1]).then_inc(ot_out, 1)
                    act.wait_ge(ot_out, 2 * h + 2)
                    act.dma_start(oa_d[bass.ds(h, 1)].rearrange("a p n -> (a p) n"), at[:]).then_inc(oa_st, 16)
                    act.wait_ge(nd_out, 3 * h + 3)
                    for c in range(TT):
                        act.activation(sqj[:], nd[:, c, 0:DV], ACT.Square, accum_out=ssm[:, c:c + 1]).then_inc(ssm_done, 1)
                        act.wait_ge(ssm_done, TT * h + c + 1)
                if s == 14:
                    act.wait_ge(varm, h + 1)
                    act.activation(d2[:], d2[:], ACT.Sqrt).then_inc(stdm, 1)
                if s == 15:
                    act.wait_ge(obt, 2 * h + 2)
                    act.dma_start(ob_d[bass.ds(h, 1)].rearrange("a p n -> (a p) n"), osig[:]).then_inc(ob_st, 16)

            def head_round(h, att):
                for s in range(SLOTS):
                    for k in UNITS_AT[s]:
                        if k % 2 == 0:
                            kq_wait(h, k // 2)
                            units_of_round(h, k)
                    attend(att, s)
                    for k in UNITS_AT[s]:
                        evac(h * HB + k // 2, k % 2)

            head_round(1, 0)
            with act.Fori(2, NH) as h:
                head_round(h, h - 1)
            for s in range(SLOTS):
                n = N_GATE + s
                split_hi(n + 1, (n + 1) // 2, (n + 1) % 2)
                evac(n, 0)
                attend(NH - 1, s)
                evac(n, 1)

            def stage_hi(k, to, first):
                act.wait_ge(stg_in[k % 2], 16 * (k // 2 + 1))
                act.activation(to[:, k % KT, :], stg[k % 2][:], ACT.Copy).then_inc(stg_hi, 1)

            for k in range(KT):
                stage_hi(k, r2h, None)
            for j in range(2 * KT):
                n = N_PA + j
                split_hi(n + 1, (n + 1) // 2, (n + 1) % 2)
                for i in range(2):
                    act.wait_ge(g_in[i], 16 * j + 16)
                    act.activation(gt[i][:], gt[i][:], ACT.Sigmoid).then_inc(g_sig, 1)
                if j < KT:
                    stage_hi(KT + j, r1h, None)
                else:
                    for i in range(2):
                        k = j - KT
                        act.wait_ge(m_sum, 2 * k + i + 1)
                        act.activation(r2h[:, k, i * HALF:(i + 1) * HALF], ev[i][:], ACT.Copy).then_inc(m_hi, 1)
            for k in range(KT):
                n = N_WO + k
                split_hi(n + 1, (n + 1) // 2, (n + 1) % 2)
                for i in range(2):
                    m = 2 * k + i
                    act.wait_ge(res_done, 2 * k + i + 1)
                    wait(act, sq_used, m - 1 if k else 0)
                    if k == 0:
                        act.wait_ge(g_used, 4 * KT)
                    act.activation(sq1[i][:], res[:, k, i * HALF:(i + 1) * HALF], ACT.Square).then_inc(sq_ready, 1)
            norm_root(0, rstd1)
            norm_hi(0, nt1, None)

            def ff_group(g, last):
                for b in range(2 * KT):
                    n = g * (2 * KT) + N_FF + b
                    if not (last and b == 2 * KT - 1):
                        split_hi(n + 1, g * KT + N_FF // 2 + (b + 1) // 2, (b + 1) % 2)
                    if b < KT:
                        for i in range(2):
                            u = g * (2 * KT) + 2 * b + i
                            act.wait_ge(gemm_done, 2 * n + i + 1)
                            act.activation(ru[i][:], gp[i][:], ACT.Relu).then_inc(r_ready, 1)
                            act.wait_ge(u_ready, u + 1)
                            act.activation(r2h[:, b, i * HALF:(i + 1) * HALF], ut[i][:], ACT.Copy).then_inc(u_hi, 1)

            with act.Fori(0, GROUPS - 1) as g:
                ff_group(g, False)
            ff_group(GROUPS - 1, True)
            act.wait_ge(ff_done, 2 * KT * GROUPS)
            squares(1, res, sq1)
            norm_root(1, rstd1)
            for t in range(TT):
                act.wait_ge(ft_tr, 2 * t + 1)
                if t >= 2:
                    act.wait_ge(out_st[t % 2], 16 * (t // 2))
                act.activation(otok[t % 2][:, 0:HALF], sbank[:, 2 * (t % 2), :], ACT.Copy).then_inc(ft_out, 1)
                act.wait_ge(ft_tr, 2 * t + 2)
                act.activation(otok[t % 2][:, HALF:], sbank[:, 2 * (t % 2) + 1, :], ACT.Copy).then_inc(ft_out, 1)

        @block.vector
        def _(dve):
            pro = Chain(dve, pdv, 0)
            ones_like = dve.memset(ones[:], 1.0)
            ones_like.then_inc(init_done, 1)
            for t in range(TT + 2):
                if t < TT:
                    dve.wait_ge(ss_ready, t + 1)
                    dve.tensor_scalar(rstd0[:, t:t + 1], ss[:, t:t + 1], 1.0 / D, EPS, ALU.mult, ALU.add).then_inc(x_var, 1)
                if 1 <= t <= TT:
                    r = rstd0[:, t - 1:t]
                    dve.wait_ge(x_std, t)
                    dve.reciprocal(r, r).then_inc(x_rstd, 1)
                    dve.wait_ge(x_rstd, t)
                    if t == 1:
                        dve.wait_ge(nwb_in, 16)
                    xt = xtok[(t - 1) % XB]
                    dve.scalar_tensor_tensor(xt[:], xt[:], r, nwb[:], ALU.mult, ALU.mult).then_inc(x_scaled, 1)
                if t >= 2:
                    for i in range(2):
                        ch = slice((t - 2) * P, (t - 1) * P)
                        dve.wait_ge(x_hi, 2 * (t - 2) + i + 1)
                        dve.tensor_tensor(r1l[:, 4 * i:4 * i + 4, ch], (tr, ob)[i][:].rearrange("p (k n) -> p k n", k=4),
                                          r1h[:, 4 * i:4 * i + 4, ch].bitcast(F32), ALU.subtract).then_inc(x_lo, 1)

            def norm_scale(stage, src, nt, rstd, final=False):
                for i in range(2):
                    r = rstd[:, i * HALF:(i + 1) * HALF]
                    dve.wait_ge(sq_used, 2 * KT * (stage + 1) - 1 + i)
                    dve.tensor_scalar(r, sbank[:, i, :], 1.0 / D, EPS, ALU.mult, ALU.add).then_inc(var_ready, 1)
                for i in range(2):
                    r = rstd[:, i * HALF:(i + 1) * HALF]
                    dve.wait_ge(std_ready, 2 * stage + i + 1)
                    dve.reciprocal(r, r).then_inc(rstd_ready, 1)
                dve.wait_ge(rstd_ready, 2 * stage + 2)
                for k in range(KT):
                    for i in range(2):
                        t = slice(i * HALF, (i + 1) * HALF)
                        if final:
                            dve.scalar_tensor_tensor(src[:, k, t], src[:, k, t], nw[:, stage, k:k + 1], rstd[:, t],
                                                     ALU.mult, ALU.mult).then_inc(fin_ready, 1)
                        else:
                            m = 2 * KT * stage + 2 * k + i
                            wait(dve, n_lo, m - 1 if k else 0)
                            dve.scalar_tensor_tensor(nt[i][:], src[:, k, t], nw[:, stage, k:k + 1], rstd[:, t],
                                                     ALU.mult, ALU.mult).then_inc(nt_ready, 1)

            dve.memset(ckq[:, 0:CONV - 1], 0.0)
            dve.memset(qpad[DK:P, :], 0.0)
            dve.memset(sg[:, 3 * P:], 0.0)
            dve.memset(cst[:], 0.0)
            pro.link(dve.memset(v1[:, :, DV:DV + 1], 1.0))
            pro.link(dve.memset(v1[:, :, DV + 1:VW], 0.0))
            two_pi = (6.28125, 0.0019350051879882812, 3.0197994998e-07)
            dve.wait_ge(c2_in, 16 * 4)
            dve.tensor_copy(identr[:], ident[:])
            pro.link(dve.tensor_copy(mask[:], sg[:, 0:3 * P]))
            pro.link(dve.tensor_copy(kqs[:], cosT[:].bitcast(I32)))
            ang = kqs[:]
            pro.link(dve.tensor_scalar(ang, ang, inv[:, 0:1], None, ALU.mult))
            for tab, turns, shift in ((sinT, cosT[:], 0.0), (cosT, sg[:], 0.25)):
                pro.link(dve.tensor_scalar(turns, ang, 1.0 / (2 * np.pi), shift, ALU.mult, ALU.add))
                pro.link(dve.tensor_scalar(turns, turns, 12582912.0, -12582912.0, ALU.add, ALU.add))
                src = ang
                for part in two_pi:
                    pro.link(dve.scalar_tensor_tensor(tab[:], turns, -part, src, ALU.mult, ALU.add))
                    src = tab[:]
                pro.link(dve.tensor_scalar(tab[:], tab[:], shift * 2 * np.pi, 3.1415925, ALU.add, ALU.min))
                dve.tensor_scalar(tab[:], tab[:], -3.1415925, None, ALU.max).then_inc(ang_ready, 1)
            dve.wait_ge(c_in, 16 * 19)
            lv = lamt[:].rearrange("p (a b n) -> p a b n", a=2, b=2)
            pro.link(dve.tensor_tensor(lv[:, :, 0, :], lv[:, :, 0, :], lv[:, :, 1, :], ALU.mult))
            dve.tensor_reduce(lams[:, 0:2], lv[:, :, 0, :], AX_X, ALU.add).then_inc(lam_ready, 1)
            pro.link(dve.tensor_scalar(aw[:], aw[:], 1.0 - LAMBDA_INIT, None, ALU.mult))
            for i in range(2):
                t = slice(i * HALF, (i + 1) * HALF)
                dve.wait_ge(if_done, i + 1)
                dve.tensor_scalar(ga[0:NH, t], sbank[0:NH, i, :], gb[0:NH, 0:1], None, ALU.add)
                pro.link(dve.tensor_scalar(ga[32:32 + NH, t], sbank[32:32 + NH, i, :], gb[32:32 + NH, 0:1], None, ALU.add))
            dve.tensor_copy(irow[:], ga[0:NH, :])
            pro.link(dve.tensor_copy(frow[:], ga[32:32 + NH, :]))
            dve.scalar_tensor_tensor(erow[:], frow[:], -1.0, frow[:], ALU.mult, ALU.min).then_inc(nf_ready, 1)
            dve.wait_ge(ln_ready, 1)
            pro.link(dve.scalar_tensor_tensor(frow[:], frow[:], 0.0, erow[:], ALU.min, ALU.subtract))
            dve.tensor_tensor_scan(mrow[:], frow[:], irow[:], 0.0, ALU.add, ALU.max)
            pro.link(dve.tensor_tensor_scan(brow[:], carry[:], frow[:], 0.0, ALU.mult, ALU.add))
            pro.link(dve.memset(yrow[:], 0.0))
            c3 = lambda r: r[:].rearrange("p (c n) -> p c n", c=TT)
            y3 = yrow[:].rearrange("p (c n) -> p c n", c=TT)
            pro.link(dve.tensor_tensor(urow[:], brow[:], mrow[:], ALU.subtract))
            pro.link(dve.tensor_tensor(irow[:], irow[:], brow[:], ALU.subtract))
            pro.link(dve.memset(mprev[:, 0:1], 0.0))
            pro.link(dve.tensor_copy(mprev[:, 1:TT], c3(mrow)[:, 0:TT - 1, P - 1]))
            dve.tensor_copy(yrow[0:NH, :], irow[:])
            dve.tensor_tensor(y3[32:32 + NH], c3(urow), mprev[:, :].unsqueeze(2).broadcast_to([NH, TT, P]), ALU.add)
            dve.tensor_tensor(y3[64:64 + NH], c3(irow), c3(urow)[:, :, P - 1:P].broadcast_to([NH, TT, P]), ALU.add)
            dve.tensor_scalar(yrow[96:96 + NH, :], mrow[:], -1.0, None, ALU.mult).then_inc(rows_ready, 1)
            dve.wait_ge(lam_exp, 1)
            pro.link(dve.tensor_tensor(lams[:, 0:1], lams[:, 3:4], lams[:, 2:3], ALU.subtract))
            pro.link(dve.tensor_scalar(neglam[:], lams[:, 0:1], -LAMBDA_INIT, None, ALU.add))
            dve.wait_ge(tk_done, 1)
            dve.wait_ge(uw_st, 32)
            for i in range(2):
                dve.wait_ge(xt_st[i], 16 * (TT // 2))
            dve.wait_ge(tab_ready, 2)
            dve.sem_inc(init_done, 2)

            chain = Chain(dve, dve_chain, DVE_HEAD)

            def attend(h, s):
                if s == 0:
                    chain.start(h * DVE_HEAD)
                    for x_, turned, s_in in ((kraw, kqs, k_in), (qraw, sg, q_in)):
                        dve.wait_ge(s_in, 16 * 5 * (h + 1))
                        dve.tensor_tensor(turned[:], turned[:], sinT[:], ALU.mult)
                        chain.link(dve.tensor_tensor(x_[:], x_[:], cosT[:], ALU.mult))
                        dve.tensor_tensor(x_[:], x_[:], turned[:], ALU.add).then_inc(roped, 1)
                    for i in range(2):
                        dve.wait_ge(v_hi, 2 * h + i + 1)
                        src = (tr, ob)[i][:].rearrange("p (t n) -> p t n", t=4)
                        dve.tensor_tensor(vs[:, 4 * i:4 * i + 4, DV:2 * DV], src, vs[:, 4 * i:4 * i + 4, 0:DV].bitcast(F32),
                                          ALU.subtract).then_inc(v_lo, 1)
                if s == 1:
                    for c, (x_, to) in enumerate(((kraw, ka), (qraw, qs))):
                        dve.wait_ge(qk_hi, 4 * h + 2 * c + 2)
                        dve.tensor_tensor(to[DK:P, 0, :], x_[0:DK, :], to[0:DK, 0, :].bitcast(F32), ALU.subtract).then_inc(qk_lo, 1)
                        dve.tensor_tensor(to[0:DK, 1, :], x_[DK:P, :], to[DK:P, 1, :].bitcast(F32), ALU.subtract).then_inc(qk_lo, 1)
                i = s - 5
                if 0 <= i < TT:
                    dve.wait_ge(o_right, TT * h + i + 1)
                    dve.tensor_tensor(oo[:, i, :], ob[:, 0:DV], otmp[:], ALU.add).then_inc(o_add, 1)

                def low(i, second):
                    dve.wait_ge(a_hi, 12 * h + tr_index(i, second) + 1)
                    j0, j1 = (4, i + 1) if second else (0, min(4, i + 1))
                    dve.tensor_tensor(atl[:, j0:j1, :], tr[:, 0:(j1 - j0) * P].rearrange("p (j n) -> p j n", n=P),
                                      ath[:, j0:j1, :].bitcast(F32), ALU.subtract).then_inc(a_lo, 1)

                if 0 <= s - 4 < TT:
                    low(s - 4, False)
                i = s - 3
                if 0 <= i < TT:
                    for c in range(2):
                        dve.wait_ge(s_done, 2 * (TT * h + i) + c + 1)
                        m = dve.tensor_reduce(mx[:, c:c + 1], sp_[:, c, 0:(i + 1) * P], AX_X, ALU.max)
                    chain.link(m)
                    dve.tensor_scalar(nb[:], mx[:], -SCALE, None, ALU.mult).then_inc(nb_ready, 1)
                if 4 <= s - 4 < TT:
                    low(s - 4, True)
                if s == 3:
                    dve.wait_ge(kq_in, 16 * h + 16)
                    dve.wait_ge(hk_ready, 4 * h + 4)
                if 3 <= s < 3 + CONV:
                    j = CONV - 1 - (s - 3)
                    src = ckq[:, j:j + S]
                    if s == 3:
                        m = dve.tensor_scalar(kqs[:], src, hc[:, j:j + 1], hc[:, CONV:CONV + 1], ALU.mult, ALU.add)
                    else:
                        m = dve.scalar_tensor_tensor(kqs[:], src, hc[:, j:j + 1], kqs[:], ALU.mult, ALU.add)
                    if j == 0:
                        m.then_inc(conv_done, 1)
                    else:
                        chain.link(m)
                if 0 <= i < TT:
                    dve.wait_ge(exp_done, 2 * (TT * h + i) + 2)
                    if i == 0:
                        wait(dve, oa_st, 16 * h)
                    chain.link(dve.reciprocal(rr[:, i, :], rs[:, i, :]))
                    chain.link(dve.tensor_scalar(cc[:], rs[:, i, 0:1], rr[:, i, 1:2], neglam[:, 0:1], ALU.mult, ALU.mult))
                    if i:
                        dve.wait_ge(tr_done, 12 * h + tr_last(i - 1) + 1)
                    dve.scalar_tensor_tensor(at[:, 0:(i + 1) * P], pr[:, 1, 0:(i + 1) * P], cc[:, 0:1],
                                             pr[:, 0, 0:(i + 1) * P], ALU.mult, ALU.add).then_inc(a_done, 1)
                if s == 6:
                    dve.wait_ge(e_exp, TT * h + TT)
                    e3 = ee[:].rearrange("p (c n) -> p c n", c=TT)
                    dve.tensor_tensor(e3, e3, keep[:, :].unsqueeze(1).broadcast_to([P, TT, P]), ALU.min).then_inc(e_sel, 1)
                if s == 11:
                    dve.wait_ge(st_done, h + 1)
                    dve.wait_ge(e_sel, h + 1)
                    for i in range(2):
                        t = slice(i * HALF, (i + 1) * HALF)
                        dve.tensor_tensor(ee[:, t], sp_[:, 0, t], ee[:, t], ALU.mult).then_inc(pt_done, 1)
                    dve.wait_ge(kt_done, h + 1)
                    for i in range(2):
                        t = slice(4 * i, 4 * i + 4)
                        dve.tensor_tensor(ckw[:, t, :], sbank[:, 2 + i, :].rearrange("p (c n) -> p c n", c=4),
                                          hk[:, t, 2:3].broadcast_to([P, 4, P]), ALU.mult).then_inc(kw_done, 1)
                if s == 12:
                    dve.wait_ge(kv_done, h + 1)
                    chain.link(dve.tensor_copy(cst[0:DK, 1, :], nd_at(0)[0:DK]))
                    for c in range(1, TT - 1):
                        m = dve.scalar_tensor_tensor(cst[0:DK, c + 1, :], cst[0:DK, c, :], hd[0:DK, c:c + 1],
                                                     nd_at(c)[0:DK], ALU.mult, ALU.add)
                        if c < TT - 2:
                            chain.link(m)
                    m.then_inc(c_done, 1)
                    r0 = rr[:, :, 0]
                    dve.wait_ge(sso_done, TT * h + TT)
                    chain.link(dve.tensor_tensor(t8[:], r0, r0, ALU.mult))
                    chain.link(dve.tensor_tensor(t8[:], t8[:], sso[:], ALU.mult))
                    dve.tensor_scalar(t8[:], t8[:], 1.0 / DV, EPS, ALU.mult, ALU.add).then_inc(varo, 1)
                    dve.wait_ge(stdo, h + 1)
                    chain.link(dve.reciprocal(rsc[:], t8[:]))
                    chain.link(dve.tensor_tensor(rsc[:], rsc[:], r0, ALU.mult))
                    dve.tensor_tensor(oo[:], oo[:], rsc[:].unsqueeze(2).broadcast_to([P, TT, DV]), ALU.mult).then_inc(osc, 1)
                if s == 14:
                    dve.wait_ge(nd_out, 3 * h + 3)
                    den = nd[:, :, DV]
                    chain.link(dve.scalar_tensor_tensor(d1[:], den, -1.0, den, ALU.mult, ALU.max))
                    chain.link(dve.tensor_tensor(d1[:], d1[:], hk[:, :, 3], ALU.max))
                    chain.link(dve.reciprocal(rm[:], d1[:]))
                    chain.link(dve.tensor_tensor(d2[:], rm[:], rm[:], ALU.mult))
                    dve.wait_ge(ssm_done, TT * h + TT)
                    chain.link(dve.tensor_tensor(d2[:], d2[:], ssm[:], ALU.mult))
                    dve.tensor_scalar(d2[:], d2[:], 1.0 / DV, EPS, ALU.mult, ALU.add).then_inc(varm, 1)
                    dve.wait_ge(stdm, h + 1)
                    chain.link(dve.reciprocal(d1[:], d2[:]))
                    chain.link(dve.tensor_tensor(rm[:], rm[:], d1[:], ALU.mult))
                    dve.tensor_tensor(nd[:, :, 0:DV], nd[:, :, 0:DV], rm[:].unsqueeze(2).broadcast_to([P, TT, DV]),
                                      ALU.mult).then_inc(hm_ready, 1)
                if s == 15:
                    dve.wait_ge(os_ready, h + 1)
                    for i in range(2):
                        t = slice(i * HALF, (i + 1) * HALF)
                        dve.wait_ge(hm_tr, 2 * h + i + 1)
                        dve.scalar_tensor_tensor(osig[:, t], (tr, ob)[i][:], hw[:, 0:1], osig[:, t], ALU.mult,
                                                 ALU.mult).then_inc(obt, 1)
                    assert chain.count == DVE_HEAD, chain.count

            for s in range(SLOTS):
                attend(0, s)
            with dve.Fori(1, NH) as h:
                for s in range(SLOTS):
                    attend(h, s)

            for j in range(2 * KT):
                n = N_PA + j
                for i in range(2):
                    k = j % KT
                    t = slice(i * HALF, (i + 1) * HALF)
                    dve.wait_ge(gemm_done, 2 * n + i + 1)
                    dve.wait_ge(g_sig, 2 * j + i + 1)
                    if j == 0 and i == 0:
                        dve.wait_ge(ob_st, 16 * NH)
                    if j < KT:
                        dve.tensor_tensor(res[:, k, t], gp[i][:], gt[i][:], ALU.mult).then_inc(gp_free, 1)
                        dve.wait_ge(gp_free, 2 * n + i + 1)
                        dve.sem_inc(g_used, 1)
                    else:
                        if j == KT:
                            dve.wait_ge(st[i], 16 * N_PA)
                        dve.tensor_tensor(gt[i][:], gp[i][:], gt[i][:], ALU.mult).then_inc(gp_free, 1)
                        dve.wait_ge(gp_free, 2 * n + i + 1)
                        wait(dve, m_lo, 2 * k + i - 1)
                        dve.tensor_tensor(ev[i][:], gt[i][:], res[:, k, t], ALU.add).then_inc(m_sum, 1)
                        dve.wait_ge(m_sum, 2 * k + i + 1)
                        dve.sem_inc(g_used, 1)
            for k in range(KT):
                for i in range(2):
                    t = slice(i * HALF, (i + 1) * HALF)
                    n = N_WO + k
                    dve.wait_ge(gemm_done, 2 * n + i + 1)
                    dve.wait_ge(res_in, 16 * KT)
                    dve.tensor_tensor(res[:, k, t], gp[i][:], res[:, k, t], ALU.add).then_inc(gp_free, 1)
                    dve.wait_ge(gp_free, 2 * n + i + 1)
                    dve.sem_inc(res_done, 1)
            norm_scale(0, res, nt1, rstd1)

            def ff_group(g):
                for b in range(2 * KT):
                    n = g * (2 * KT) + N_FF + b
                    for i in range(2):
                        t = slice(i * HALF, (i + 1) * HALF)
                        u = g * (2 * KT) + 2 * b + i
                        if b < KT:
                            dve.wait_ge(r_ready, u + 1)
                            dve.scalar_tensor_tensor(ut[i][:], gp[i][:], 0.0, ru[i][:], ALU.max, ALU.mult).then_inc(gp_free, 1)
                            dve.wait_ge(gp_free, 2 * n + i + 1)
                            dve.sem_inc(u_ready, 1)
                            dve.wait_ge(u_hi, u + 1)
                            dve.tensor_tensor(r2l[:, b, t], ut[i][:], r2h[:, b, t].bitcast(F32), ALU.subtract).then_inc(u_lo, 1)
                        else:
                            k = b - KT
                            dve.wait_ge(gemm_done, 2 * n + i + 1)
                            dve.tensor_tensor(res[:, k, t], gp[i][:], res[:, k, t], ALU.add).then_inc(gp_free, 1)
                            dve.wait_ge(gp_free, 2 * n + i + 1)
                            dve.sem_inc(ff_done, 1)

            with dve.Fori(0, GROUPS) as g:
                ff_group(g)
            norm_scale(1, res, None, rstd1, final=True)

        @block.gpsimd
        def _(pool):
            def split_lo(n, slot):
                pool.wait_ge(w_hi, n + 1)
                pool.tensor_tensor(wl[slot][:], raw[slot][:], wh[slot][:].bitcast(F32), ALU.subtract).then_inc(w_split, 1)

            def norm_lo(stage, nt):
                for k in range(KT):
                    for i in range(2):
                        t = slice(i * HALF, (i + 1) * HALF)
                        pool.wait_ge(n_hi, 2 * KT * stage + 2 * k + i + 1)
                        pool.tensor_tensor(r1l[:, k, t], nt[i][:], r1h[:, k, t].bitcast(F32), ALU.subtract).then_inc(n_lo, 1)

            pool.memset(wifh[:].bitcast(F32), 0.0).then_inc(wif_set, 1)
            pool.memset(wifl[:].bitcast(F32), 0.0).then_inc(wif_set, 1)
            pool.dma_start(cosT[:].bitcast(I32), positions[0].partition_broadcast(P)).then_inc(c2_in, 16)
            pool.dma_start(inv[:], c_inv).then_inc(c2_in, 16)
            pool.dma_start(sg[:, 0:3 * P], c_mask).then_inc(c2_in, 16)
            pool.dma_start(keep[:], c_keep).then_inc(c2_in, 16)
            pool.wait_ge(wif_h, 2)
            pool.tensor_tensor(wifl[:, :, 0:NH], wif[:, :, 0:NH], wifh[:, :, 0:NH].bitcast(F32), ALU.subtract)
            pool.tensor_tensor(wifl[:, :, 32:32 + NH], wif[:, :, NH:2 * NH], wifh[:, :, 32:32 + NH].bitcast(F32),
                               ALU.subtract).then_inc(wif_l, 1)
            split_lo(0, 0)
            for b in range(HB):
                split_lo(b + 1, (b + 1) % 2)
            pool.wait_ge(c2_in, 16 * 4)
            pool.wait_ge(tk_done, 1)
            pool.wait_ge(c_in, 16 * 19)

            def attend(h, s):
                if s == 2:
                    wait(pool, obt, 2 * h)
                    pool.tensor_copy(hk[:], tk[:, :, :, bass.ds(h, 1)].rearrange("p c q a -> p c (q a)")).then_inc(hk_ready, 1)
                    pool.tensor_copy(hd[:], dc[:, :, bass.ds(h, 1)].rearrange("p c a -> p (c a)")).then_inc(hk_ready, 1)
                    pool.tensor_copy(hc[:], cw[:, :, bass.ds(h, 1)].rearrange("p c a -> p (c a)")).then_inc(hk_ready, 1)
                    pool.tensor_copy(hw[:], mlw[:, bass.ds(h, 1)]).then_inc(hk_ready, 1)
                if s == 8:
                    pool.wait_ge(sg_ready, h + 1)
                    pool.tensor_tensor(kqs[:], kqs[:], sg[:], ALU.mult).then_inc(kq_ready, 1)
                if s == 12:
                    pool.wait_ge(st_done, h + 1)
                    pool.wait_ge(i_in, 16 * h + 16)
                    pool.tensor_tensor(qpad[0:DK, :], qpad[0:DK, :], kraw[0:DK, :], ALU.mult).then_inc(qi_ready, 1)

            def head_round(h, att):
                for s in range(SLOTS):
                    for k in UNITS_AT[s]:
                        if k % 2:
                            continue
                        split_lo(h * HB + k // 2 + 1, (k // 2 + 1) % 2)
                    attend(att, s)

            head_round(1, 0)
            with pool.Fori(2, NH) as h:
                head_round(h, h - 1)
            for s in range(SLOTS):
                n = N_GATE + s
                split_lo(n + 1, (n + 1) % 2)
                attend(NH - 1, s)

            def stage_lo(k, hi, lo):
                pool.wait_ge(stg_hi, k + 1)
                pool.tensor_tensor(lo[:, k % KT, :], stg[k % 2][:], hi[:, k % KT, :].bitcast(F32), ALU.subtract).then_inc(stg_lo, 1)

            for k in range(KT):
                stage_lo(k, r2h, r2l)
            for j in range(2 * KT):
                n = N_PA + j
                split_lo(n + 1, (n + 1) % 2)
                if j < KT:
                    stage_lo(KT + j, r1h, r1l)
                else:
                    for i in range(2):
                        k = j - KT
                        t = slice(i * HALF, (i + 1) * HALF)
                        pool.wait_ge(m_hi, 2 * k + i + 1)
                        pool.tensor_tensor(r2l[:, k, t], ev[i][:], r2h[:, k, t].bitcast(F32), ALU.subtract).then_inc(m_lo, 1)
            for k in range(KT):
                n = N_WO + k
                split_lo(n + 1, (n + 1) % 2)
            norm_lo(0, nt1)

            with pool.Fori(0, GROUPS - 1) as g:
                for b in range(2 * KT):
                    split_lo(g * (2 * KT) + N_FF + b + 1, (b + 1) % 2)
            for b in range(2 * KT - 1):
                split_lo((GROUPS - 1) * 2 * KT + N_FF + b + 1, (b + 1) % 2)


def shape_constants():
    inv = (500000.0 ** (-np.arange(0, 16, 2, dtype=np.float32) / 16)).astype(np.float32)
    col = np.zeros((P, 1), np.float32)
    for base in (0, DK):
        col[base:base + 8, 0] = -inv
        col[base + 8:base + 16, 0] = inv
    mask = np.zeros((P, 3 * P), np.float32)
    mask[:, P:2 * P][np.arange(P)[None, :] > np.arange(P)[:, None]] = NEG
    last = np.zeros((P, P), np.float32)
    last[P - 1, :] = 1.0
    carry = np.ones((NH, S), np.float32)
    carry[:, ::P] = 0.0
    keep = np.where(np.arange(P)[None, :] >= np.arange(P)[:, None], np.float32(3e38), np.float32(0))
    return {"c_ident": np.eye(P, dtype=np.float32), "c_inv": col, "c_mask": mask,
            "c_last": last, "c_carry": carry, "c_keep": keep}


_INS = ["x", "positions", "norm_mix_w", "w_in", "ml_gate_b", "conv_w", "conv_b", "da_lambda", "da_subln_w",
        "ml_norm_w", "w_proj_a", "w_proj_b", "w_out", "norm_ffn_w", "w_ff1", "w_ff2", "final_norm_w"]
_CONSTS = ["c_ident", "c_inv", "c_mask", "c_last", "c_carry", "c_keep"]


def kernel(**inputs):
    import concourse.bacc as _bacc
    from concourse.bass_utils import run_bass_kernel_spmd as _run

    nc = _bacc.Bacc("TRN2", target_bir_lowering=False, num_devices=1)
    arrays, args = {}, []
    consts = shape_constants()
    for name in _INS + _CONSTS:
        a = np.ascontiguousarray(consts[name] if name in consts else inputs[name])
        arrays[f"in_{name}"] = a
        args.append(nc.dram_tensor(f"in_{name}", a.shape, mybir.dt.from_np(a.dtype), kind="ExternalInput").ap())
    out = nc.dram_tensor("out_0", (1, S, D), F32, kind="ExternalOutput").ap()
    build(nc, *args, out)
    r = _run(nc, [arrays], core_ids=[0])
    return r.results[0]["out_0"]
```

```python
from contextlib import ExitStack

import numpy as np

import concourse.bass as bass
from concourse import mybir

P = 128
F32 = mybir.dt.float32
F32R = mybir.dt.float32r
I32 = mybir.dt.int32
ALU = mybir.AluOpType
ACT = mybir.ActivationFunctionType
AX_X = mybir.AxisListType.X

D = 1024
S = 1024
KT = D // P
TT = S // P
HALF = S // 2
NH = 8
DK = 64
DV = 128
CONV = 4
DFF = 4 * D
EPS = 1e-6
LAMBDA_INIT = 0.2
SCALE = DK ** -0.5
NEG = -float(2 ** 100)
VW = DV + 2

OFF_Q, OFF_K, OFF_V = 0, 1024, 2048
OFF_MQ, OFF_MK, OFF_MV = 3072, 3584, 4096
OFF_I, OFF_F, OFF_O, OFF_G = 5120, 5128, 5136, 6160

HB = 6
N_GATE = NH * HB
N_PA = N_GATE + 16
N_PB = N_PA + KT
N_WO = N_PB + KT
N_FF = N_WO + KT
GROUPS = DFF // (KT * P)
N_LAST = N_FF + (2 * GROUPS - 1) * KT

X_RAW = 2
XB = 4

SLOTS = 16
QUARTERS = (4, 4, 5, 0, 3, 2, 3, 3, 4, 4, 4, 4, 2, 2, 4, 0)


def part_slots(quarters):
    at = [s for s, n in enumerate(quarters) for _ in range(n)]
    starts = [[k for k in range(2 * HB) if at[4 * k] == s] for s in range(SLOTS)]
    ends = [[k for k in range(2 * HB) if at[4 * k + 3] == s] for s in range(SLOTS)]
    return at, starts, ends


QUARTER_AT, STARTS_AT, ENDS_AT = part_slots(QUARTERS)
GATE_UNITS_AT = [[k for k in range(24) if k * SLOTS // 24 == s] for s in range(SLOTS)]
STAGE_AT = {12: (0, 1), 13: (2, 3), 14: (4, 5), 15: (6, 7)}


def wait(eng, sem, value):
    if isinstance(value, int) and value <= 0:
        return
    eng.wait_ge(sem, value)


def tr_index(i, second):
    return i + max(0, i - 4) + (1 if second else 0)


def tr_last(i):
    return tr_index(i, i >= 4)


class Chain:

    def __init__(self, eng, sem):
        self.eng, self.sem = eng, sem
        self.base, self.count = 0, 0

    def start(self, base):
        self.base, self.count = base, 0

    def link(self, ins):
        self.count += 1
        ins.then_inc(self.sem, 1)
        self.eng.wait_ge(self.sem, self.base + self.count)


def build(nc, x, positions, norm_mix_w, w_in, ml_gate_b, conv_w, conv_b, da_lambda, da_subln_w,
          ml_norm_w, w_proj_a, w_proj_b, w_out, norm_ffn_w, w_ff1, w_ff2, final_norm_w,
          c_ident, c_inv, c_mask, c_last, c_carry, c_keep, out):
    x2 = x[0]
    out2 = out[0]
    w_in2, w_pa, w_pb, w_o, w_f1, w_f2 = w_in[0], w_proj_a[0], w_proj_b[0], w_out[0], w_ff1[0], w_ff2[0]

    proj_d = nc.dram_tensor("proj_d", (N_PA, P, S), F32, kind="Internal").ap()
    xT_d = nc.dram_tensor("xT_d", (KT, P, S), F32, kind="Internal").ap()
    oa_d = nc.dram_tensor("oa_d", (NH, P, S), F32, kind="Internal").ap()
    ob_d = nc.dram_tensor("ob_d", (NH, P, S), F32, kind="Internal").ap()
    u_d = nc.dram_tensor("u_d", (NH, S), F32, kind="Internal").ap()
    inter_d = nc.dram_tensor("inter_d", (NH, S), F32, kind="Internal").ap()

    with ExitStack() as ctx:
        def sb(name, shape, dt=F32, scope=ctx):
            return scope.enter_context(nc.sbuf_tensor(name, shape, dt))

        def ps(name, shape):
            return ctx.enter_context(nc.psum_tensor(name, shape, F32))

        def sem(name):
            return ctx.enter_context(nc.semaphore(name))

        raw = [sb(f"w_raw{i}", [P, KT, P]) for i in range(2)]
        wh = [sb(f"w_hi{i}", [P, KT, P], F32R) for i in range(2)]
        wl = [sb(f"w_lo{i}", [P, KT, P], F32R) for i in range(2)]
        r1h = sb("r1h", [P, KT, S], F32R)
        r1l = sb("r1l", [P, KT, S], F32R)
        ev = [sb(f"ev{i}", [P, HALF]) for i in range(2)]
        ident = sb("ident", [P, P])
        ones = sb("ones", [P, P])
        nw = sb("nw", [P, 2, KT])
        tk = sb("tk", [P, TT, 4, NH])
        dc = sb("dc", [P, TT, NH])
        cw = sb("cw", [P, CONV + 1, NH])
        mlw = sb("mlw", [P, NH])
        aw = sb("aw", [P, 1])
        neglam = sb("neglam", [P, 1])

        heads = ctx.enter_context(ExitStack())
        identr = sb("identr", [P, P], F32R, heads)
        keep = sb("keep", [P, P], F32, heads)
        mask = sb("mask", [P, 3 * P], F32R, heads)
        cosT = sb("cosT", [P, S], F32, heads)
        sinT = sb("sinT", [P, S], F32, heads)
        inv = sb("inv", [P, 1], F32, heads)
        ckq = sb("ckq", [P, CONV - 1 + S], F32, heads)
        kqs = sb("kqs", [P, S], F32, heads)
        sg = sb("sg", [P, S], F32, heads)
        qpad = sb("qpad", [P, S], F32, heads)
        v1 = sb("v1", [P, TT, VW], F32, heads)
        cst = sb("cst", [P, TT, VW], F32, heads)

        with ExitStack() as sc:
            xtok = [sb(f"xtok{i}", [P, D], F32, sc) for i in range(XB)]
            nwb = sb("nwb", [P, D], F32, sc)
            ss = sb("ss", [P, TT], F32, sc)
            rstd0 = sb("rstd0", [P, TT], F32, sc)
            xTs = [sb(f"xTs{i}", [P, KT, P], F32, sc) for i in range(2)]
            wif = sb("wif", [P, KT, 16], F32, sc)
            wifh = sb("wifh", [P, KT, P], F32R, sc)
            wifl = sb("wifl", [P, KT, P], F32R, sc)
            gb = sb("gb", [P, 1], F32, sc)
            lamt = sb("lamt", [P, 4 * DK], F32, sc)
            lams = sb("lams", [P, 4], F32, sc)
            irow = sb("irow", [NH, S], F32, sc)
            frow = sb("frow", [NH, S], F32, sc)
            erow = sb("erow", [NH, S], F32, sc)
            mrow = sb("mrow", [NH, S], F32, sc)
            brow = sb("brow", [NH, S], F32, sc)
            wrow = sb("wrow", [NH, S], F32, sc)
            mprev = sb("mprev", [NH, TT], F32, sc)
            carry = sb("carry", [NH, S], F32, sc)
            yrow = sb("yrow", [P, S], F32, sc)
            last = sb("last", [P, P], F32, sc)
        ga, urow = yrow, erow

        with heads, ExitStack() as sc:
            qraw = sb("qraw", [P, S], F32, sc)
            kraw = sb("kraw", [P, S], F32, sc)
            qs = sb("qs", [P, 2, S], F32R, sc)
            ka = sb("ka", [P, 2, S], F32R, sc)
            kb = sb("kb", [P, 2, S], F32R, sc)
            vs = sb("vs", [P, TT, 2 * DV], F32R, sc)
            pr = sb("pr", [P, 2, S], F32, sc)
            at = sb("at", [P, S], F32, sc)
            at3 = sb("at3", [P, HALF], F32, sc)
            ath = sb("ath", [P, TT, P], F32R, sc)
            atl = sb("atl", [P, TT, P], F32R, sc)
            oo = sb("oo", [P, TT, DV], F32, sc)
            otmp = sb("otmp", [P, DV], F32, sc)
            sqj = sb("sqj", [P, DV], F32, sc)
            mx = sb("mx", [P, 2], F32, sc)
            nb = sb("nb", [P, 2], F32, sc)
            rs = sb("rs", [P, TT, 2], F32, sc)
            rr = sb("rr", [P, TT, 2], F32, sc)
            cc = sb("cc", [P, 1], F32, sc)
            sso = sb("sso", [P, TT], F32, sc)
            t8 = sb("t8", [P, TT], F32, sc)
            rsc = sb("rsc", [P, TT], F32, sc)
            nd = sb("nd", [P, TT, VW], F32, sc)
            osig = sb("osig", [P, S], F32, sc)
            hk = sb("hk", [P, TT, 4], F32, sc)
            hd = sb("hd", [P, TT], F32, sc)
            hc = sb("hc", [P, CONV + 1], F32, sc)
            hw = sb("hw", [P, 1], F32, sc)
            warm = sb("warm", [P, 1], F32, sc)
            ssm = sb("ssm", [P, TT], F32, sc)
            d1 = sb("d1", [P, TT], F32, sc)
            d2 = sb("d2", [P, TT], F32, sc)
            rm = sb("rm", [P, TT], F32, sc)

        def at_late(i):
            return at3[:] if i % 2 else at[:, HALF:]

        ckw = ckq[:, CONV - 1:].rearrange("p (c n) -> p c n", c=TT)
        ee = qraw

        with ExitStack() as sc:
            r2h = sb("r2h", [P, KT, S], F32R, sc)
            r2l = sb("r2l", [P, KT, S], F32R, sc)
            res = sb("res", [P, KT, S], F32, sc)
            with ExitStack() as s2:
                stg = [sb(f"stg{i}", [P, S], F32, s2) for i in range(2)]
                gt = [sb(f"gt{i}", [P, HALF], F32, s2) for i in range(2)]
            with ExitStack() as s2:
                ut = [sb(f"ut{i}", [P, HALF], F32, s2) for i in range(2)]
                acc = sb("acc", [P, S], F32, s2)
                rstd1 = sb("rstd1", [P, S], F32, s2)
                otok1 = sb("otok1", [P, D], F32, s2)
                rfin = sb("rfin", [P, TT], F32, s2)
        otok = [rstd1, otok1]
        fnb = ev

        gp = [ps(f"gp{i}", [P, HALF]) for i in range(2)]
        sp_ = ps("scores", [P, 2, S])
        tr = ps("tr", [P, 512])
        ob = ps("ob", [P, 512])
        sbank = sp_[:, :, :].rearrange("p c (b n) -> p (c b) n", b=2)

        def nd_at(c):
            return sbank[:, c // 3, (c % 3) * VW:(c % 3 + 1) * VW]

        w_loaded = [sem(f"w_loaded{i}") for i in range(2)]
        w_loaded_q = sem("w_loaded_q")
        w_hi, w_split, gemm_done, gp_free = sem("w_hi_done"), sem("w_split"), sem("gemm_done"), sem("gp_free")
        ev_ready = [sem(f"ev_ready{i}") for i in range(2)]
        st = [sem(f"proj_stored{i}") for i in range(2)]
        ident_in, c2_in = sem("ident_in"), sem("head_consts_in")
        c_in, wif_in, nwb_in, x_in = sem("consts_in"), sem("wif_in"), sem("nwb_in"), [sem(f"x_in{i}") for i in range(XB)]
        ss_ready, x_var, x_std, x_rstd, x_scaled = (sem(n) for n in ("ss_ready", "x_var", "x_std", "x_rstd", "x_scaled"))
        x_tr, x_hi, x_lo = sem("x_transposed"), sem("x_hi"), sem("x_lo")
        xts_out, xt_st = sem("xts_out"), [sem("xt_stored0"), sem("xt_stored1")]
        sq_ready, sq_used, var_ready, std_ready = sem("sq_ready"), sem("sq_used"), sem("var_ready"), sem("std_ready")
        rstd_ready, n_hi, n_lo = sem("rstd_ready"), sem("n_hi"), sem("n_lo")
        ss_done = sem("sumsq_done")
        wif_set, wif_h, wif_l, if_done = sem("wif_set"), sem("wif_h"), sem("wif_l"), sem("if_done")
        pdv, pact = sem("prologue_dve"), sem("prologue_act")
        nf_ready, ln_ready, rows_ready, wrow_ready, tk_tr, tk_ready, dc_done, tk_done = (
            sem("nf_ready"), sem("ln_ready"), sem("rows_ready"), sem("wrow_ready"), sem("tk_tr"), sem("tk_ready"),
            sem("dc_done"), sem("tk_done"))
        uw_st = sem("uw_stored")
        ang_ready, tab_ready, lam_ready, lam_exp = sem("ang_ready"), sem("tab_ready"), sem("lam_ready"), sem("lam_exp")
        init_done = sem("init_done")
        q_in, k_in, v_in, kq_in, mv_in, o_in, u_in, i_in = (sem(n) for n in (
            "q_in", "k_in", "v_in", "kq_in", "mv_in", "o_in", "u_in", "inter_in"))
        roped, qk_hi, qk_lo, kb_in = sem("roped"), sem("qk_hi"), sem("qk_lo"), sem("kb_in")
        vtr, v_hi, v_lo, mv_out = sem("vtr"), sem("v_hi"), sem("v_lo"), sem("mv_out")
        s_done, nb_ready, exp_done, a_done = sem("s_done"), sem("nb_ready"), sem("exp_done"), sem("a_done")
        tr_done, a_hi, a_lo, pv_done = sem("tr_done"), sem("a_hi"), sem("a_lo"), sem("pv_done")
        o_right, o_add, sso_done, varo, stdo, osc = (sem(n) for n in ("o_right", "o_add", "sso_done", "varo", "stdo", "osc"))
        ot_tr, ot_out, oa_st = sem("ot_tr"), sem("ot_out"), sem("oa_stored")
        hk_ready, conv_done, sg_ready, os_ready, kq_ready, qp_ready = (sem(n) for n in (
            "hk_ready", "conv_done", "sg_ready", "os_ready", "kq_ready", "qp_ready"))
        e_exp, e_sel, st_done, kt_done, pt_done, kw_done, kv_done, c_done, qi_ready = (sem(n) for n in (
            "e_exp", "e_sel", "st_done", "kt_done", "pt_done", "kw_done", "kv_done", "c_done", "qi_ready"))
        nd_done, nd_out, ssm_done, varm, stdm, hm_ready, hm_tr, obt, ob_st = (sem(n) for n in (
            "nd_done", "nd_out", "ssm_done", "varm", "stdm", "hm_ready", "hm_tr", "obt", "ob_stored"))
        dve_chain = sem("dve_chain")
        stg_in, stg_hi, stg_lo, stgb_lo = [sem("stg_in0"), sem("stg_in1")], sem("stg_hi"), sem("stg_lo_a"), sem("stg_lo_b")
        g_in, g_sig, g_used = [sem("g_in0"), sem("g_in1")], sem("g_sig"), sem("g_used")
        m_sum, m_hi, m_lo, res_in = sem("m_sum"), sem("m_hi"), sem("m_lo"), sem("res_in")
        res_done = sem("res_done")
        u_ready, u_hi, u_lo = sem("u_ready"), sem("u_hi"), sem("u_lo")
        z_ready, fin_done, fs_done, f_var, f_std, f_rstd, fnb_in = (sem(n) for n in (
            "z_ready", "fin_done", "fs_done", "f_var", "f_std", "f_rstd", "fnb_in"))
        ft_tr, ft_out, out_st = sem("ft_tr"), sem("ft_out"), [sem("out_st0"), sem("out_st1")]

        DVE_HEAD = 46

        def col_block(w, first):
            return w.rearrange("(k p) n -> p k n", p=P)[:, :, bass.ds(first, P)]

        block = ctx.enter_context(nc.Block())

        @block.sync
        def _(sp):
            def wload(n, slot, src):
                wait(sp, w_split, n - 1)
                sp.dma_start(raw[slot][:], src).then_inc(w_loaded[slot], 16)

            def wload_head(h, b):
                n = h * HB + b
                if b == 3:
                    wait(sp, w_split, n - 1)
                    for j, off in enumerate((OFF_MK, OFF_MQ)):
                        src = w_in2.rearrange("(k p) n -> p k n", p=P)[:, :, bass.ds(h * DK + off, DK)]
                        sp.dma_start(raw[1][:, :, j * DK:(j + 1) * DK], src).then_inc(
                            (w_loaded[1], w_loaded_q)[j], 16)
                else:
                    off = (OFF_Q, OFF_K, OFF_V, None, OFF_MV, OFF_O)[b]
                    wload(n, b % 2, col_block(w_in2, h * P + off))

            def store(n):
                for i in range(2):
                    sp.wait_ge(ev_ready[i], n + 1)
                    sp.dma_start(proj_d[bass.ds(n, 1), :, i * HALF:(i + 1) * HALF].rearrange("a p n -> (a p) n"),
                                 ev[i][:]).then_inc(st[i], 16)

            def head_src(h, b):
                return proj_d[bass.ds(h * HB + b, 1)].rearrange("a p n -> (a p) n")

            def turned_rows(to, src, s_in):
                for c in range(2):
                    for half in range(2):
                        a, b = c * DK + half * 8, c * DK + (1 - half) * 8
                        sp.dma_start(to[a:a + 8, :], src[b:b + 8, :]).then_inc(s_in, 16)

            def att_loads(h):
                if isinstance(h, int) and h == 0:
                    sp.wait_ge(init_done, 3)
                for i in range(2):
                    sp.wait_ge(st[i], 16 * (h * HB + 2))
                wait(sp, qi_ready, h)
                sp.dma_start(kraw[:], head_src(h, 1)).then_inc(k_in, 16)
                wait(sp, kt_done, h)
                turned_rows(kqs, head_src(h, 1), k_in)
                wait(sp, nd_done, h)
                sp.dma_start(qraw[:], head_src(h, 0)).then_inc(q_in, 16)
                wait(sp, kq_ready, h)
                turned_rows(sg, head_src(h, 0), q_in)
                for i in range(2):
                    sp.wait_ge(st[i], 16 * (h * HB + 5))
                sp.dma_start(pr[:, 0, :], head_src(h, 2)).then_inc(v_in, 16)
                sp.dma_start(pr[:, 1, :], head_src(h, 4)).then_inc(mv_in, 16)

            def ml_loads(h):
                for i in range(2):
                    sp.wait_ge(st[i], 16 * (h * HB + HB))
                wait(sp, kv_done, h)
                sp.dma_start(ckq[:, CONV - 1:], head_src(h, 3)).then_inc(kq_in, 16)
                wait(sp, ob_st, 16 * h)
                sp.dma_start(osig[:], head_src(h, 5)).then_inc(o_in, 16)

            def row_loads(h):
                sp.wait_ge(qk_lo, 4 * h + 4)
                if isinstance(h, int) and h == 0:
                    sp.wait_ge(uw_st, 32)
                for buf, src, s_in in ((qraw, u_d, u_in), (kraw, inter_d, i_in)):
                    row = src[bass.ds(h, 1), :].rearrange("a n -> (a n)").partition_broadcast(P)
                    sp.dma_start(buf[:], row).then_inc(s_in, 16)

            def stage_in(k, src):
                if k >= KT + 2:
                    sp.wait_ge(stgb_lo, k - KT - 1)
                else:
                    wait(sp, stg_lo, k - 1)
                sp.dma_start(stg[k % 2][:], src).then_inc(stg_in[k % 2], 16)

            def x_load(j):
                wait(sp, x_tr, 2 * (j - XB + 1))
                t = j % TT
                sp.dma_start(xtok[j % XB][:], x2[t * P:(t + 1) * P, :]).then_inc(x_in[j % XB], 16)

            def x_store(t):
                sp.wait_ge(xts_out, 2 * t + 2)
                sp.dma_start(xT_d[:, :, t * P:(t + 1) * P].rearrange("k p n -> p k n"), xTs[t % 2][:]).then_inc(xt_st[t % 2], 16)

            for j in range(TT + XB):
                x_load(j)
                if j == 0:
                    sp.dma_start(nwb[:], norm_mix_w[0].partition_broadcast(P)).then_inc(nwb_in, 16)
                    sp.dma_start(ident[:], c_ident).then_inc(ident_in, 16)
                if j == 3:
                    wload_head(0, 0)
                if j == 6:
                    wload_head(0, 1)
            def head_round(h, att, first=False):
                for b in range(HB):
                    if not (first and b < 2):
                        wload_head(h, b)
                    if isinstance(h, int):
                        for t in (2 * (h * HB + b) - 6, 2 * (h * HB + b) - 5):
                            if 0 <= t < TT:
                                if t + XB < TT:
                                    x_load(TT + XB + t)
                                x_store(t)
                    if isinstance(h, int) and h == 1 and b == 0:
                        sp.wait_ge(rows_ready, 1)
                        sp.dma_start(u_d, urow[:]).then_inc(uw_st, 16)
                        sp.wait_ge(wrow_ready, 1)
                        sp.dma_start(inter_d, wrow[:]).then_inc(uw_st, 16)
                    if b >= 2 or not first:
                        store(h * HB + b - 2)
                    if att is not None:
                        if b == 0:
                            att_loads(att)
                        if b == 1:
                            ml_loads(att)
                    if att is not None and b == 2:
                        row_loads(att)

            head_round(0, None, first=True)
            head_round(1, 0)
            with sp.Fori(2, NH) as h:
                head_round(h, h - 1)
            for j in range(16):
                n = N_GATE + j
                wload(n, n % 2, col_block(w_in2, OFF_G + j * P))
                if j == 13:
                    sp.wait_ge(oa_st, 16 * NH)
                    sp.wait_ge(ob_st, 16 * NH)
                for k in STAGE_AT.get(j - 1, ()):
                    stage_in(k, oa_d[k])
                store(n - 2)
                if j == 0:
                    att_loads(NH - 1)
                if j == 1:
                    ml_loads(NH - 1)
                if j == 2:
                    row_loads(NH - 1)
            for k in range(2):
                wload(N_PA + k, k, col_block(w_pa, k * P))
                for i in STAGE_AT[15] if k == 0 else ():
                    stage_in(i, oa_d[i])
                store(N_PA - 2 + k)
            for i in range(2):
                sp.wait_ge(st[i], 16 * N_PA)
            def gate_in(j):
                for i in range(2):
                    wait(sp, g_used, 2 * (j - 1) + i + 1 if j else 0)
                    sp.dma_start(gt[i][:], proj_d[N_GATE + j, :, i * HALF:(i + 1) * HALF]).then_inc(g_in[i], 16)

            for j in range(2 * KT):
                n = N_PA + j + 2
                if n < N_PB:
                    src = col_block(w_pa, (n - N_PA) * P)
                elif n < N_WO:
                    src = col_block(w_pb, (n - N_PB) * P)
                else:
                    src = col_block(w_o, (n - N_WO) * P)
                gate_in(j)
                wload(n, n % 2, src)
                if j < KT:
                    stage_in(KT + j, ob_d[j])
                else:
                    k = j - KT
                    sp.wait_ge(m_sum, 2 * k + 2)
                    sp.dma_start(res[:, k, :], xT_d[k]).then_inc(res_in, 16)
            for k in range(KT):
                n = N_WO + k + 2
                src = col_block(w_o, (n - N_WO) * P) if n < N_FF else col_block(w_f1, (n - N_FF) * P)
                wload(n, n % 2, src)

            def ff2_block(g, b):
                return w_f2.rearrange("(g k p) n -> g p k n", p=P, k=KT)[
                    bass.ds(g, 1), :, :, b * P:(b + 1) * P].rearrange("a p k n -> (a p) k n")

            def ff_loads(g, last):
                n0 = 2 * KT * g + N_FF
                for b in range(2, KT if last else 2 * KT + 2):
                    if b < KT:
                        src = col_block(w_f1, g * (KT * P) + b * P)
                    elif b < 2 * KT:
                        src = ff2_block(g, b - KT)
                    else:
                        src = col_block(w_f1, (g + 1) * (KT * P) + (b - 2 * KT) * P)
                    wload(n0 + b, b % 2, src)

            def out_store(t):
                sp.wait_ge(ft_out, 2 * t + 2)
                sp.dma_start(out2[t * P:(t + 1) * P, :], otok[t % 2][:]).then_inc(out_st[t % 2], 16)

            with sp.Fori(0, GROUPS - 1) as g:
                ff_loads(g, False)
            ff_loads(GROUPS - 1, True)
            for m in range(2 * KT):
                wload(N_LAST + m, m % 2, ff2_block(GROUPS - 1, m % KT))
                if m == 3:
                    sp.wait_ge(u_lo, 2 * KT * GROUPS)
                    for i in range(2):
                        sp.dma_start(fnb[i][:], final_norm_w[i * HALF:(i + 1) * HALF].partition_broadcast(P)).then_inc(fnb_in, 16)
                if m >= KT + 5:
                    out_store(m - KT - 5)
            for t in range(3, TT):
                out_store(t)
            for i in range(2):
                sp.wait_ge(out_st[i], 16 * (TT // 2))
            for i in range(2):
                sp.wait_ge(xt_st[i], 16 * (TT // 2))

        @block.tensor
        def _(pe):
            def unit(n, slot, half, mh, ml, before_k=None, alone=None, quarter=None):
                first = quarter in (None, 0)
                if first and (half == 0 or alone is not None):
                    pe.wait_ge(w_split, n + 1)
                if first:
                    wait(pe, gp_free, 2 * n + half - 1 if alone is None or n == N_LAST else 2 * n - 2)
                tokens = half if alone is None else alone
                t = slice(tokens * HALF, (tokens + 1) * HALF)
                for k in range(KT) if quarter is None else range(2 * quarter, 2 * quarter + 2):
                    if before_k:
                        before_k(k)
                    pe.matmul(gp[half][:], wh[slot][:, k, :], mh[:, k, t], start=(k == 0), stop=False)
                    pe.matmul(gp[half][:], wh[slot][:, k, :], ml[:, k, t], start=False, stop=False)
                    mm = pe.matmul(gp[half][:], wl[slot][:, k, :], mh[:, k, t], start=False, stop=(k == KT - 1))
                if quarter in (None, 3):
                    mm.then_inc(gemm_done, 1 if alone is None else 2)

            def x_transpose(j):
                if j < TT:
                    pe.wait_ge(x_scaled, j + 1)
                else:
                    pe.wait_ge(x_in[j % XB], 16 * (j // XB + 1))
                for i in range(2):
                    if j <= TT:
                        wait(pe, x_lo, 2 * (j - 1) + i + 1 if j else 0)
                    else:
                        pe.wait_ge(xts_out, 2 * (j - TT - 1) + i + 1)
                    for n in range(4):
                        k = 4 * i + n
                        mm = pe.transpose([tr, ob][i][:, n * P:(n + 1) * P], xtok[j % XB][:, k * P:(k + 1) * P], ident[:])
                    mm.then_inc(x_tr, 1)

            def gates_half(i, tiles):
                t = slice(i * HALF, (i + 1) * HALF)
                for k in range(KT):
                    if k in tiles:
                        x_transpose(tiles[k])
                    if k == 0:
                        pe.wait_ge(x_lo, TT * (i + 1))
                        pe.wait_ge(wif_l, 1)
                    pe.matmul(sbank[:, i, :], wifh[:, k, :], r1h[:, k, t], start=(k == 0), stop=False)
                    pe.matmul(sbank[:, i, :], wifh[:, k, :], r1l[:, k, t], start=False, stop=False)
                    mm = pe.matmul(sbank[:, i, :], wifl[:, k, :], r1h[:, k, t], start=False, stop=(k == KT - 1))
                mm.then_inc(if_done, 1)

            pe.wait_ge(ident_in, 16)
            for j in range(4):
                x_transpose(j)
            gates_half(0, {2: 4, 6: 5})
            unit(0, 0, 0, r1h, r1l, before_k=lambda k: x_transpose(6 + k // 4) if k in (2, 6) else None)
            gates_half(1, {})

            def head_unit(h, k, quarter=None):
                b = k // 2
                unit(h * HB + b, b % 2, k % 2, r1h, r1l, quarter=quarter)

            for k in range(2 * HB):
                if k:
                    head_unit(0, k)
                if X_RAW <= k < X_RAW + TT:
                    x_transpose(TT + k - X_RAW)
                if k == 7:
                    pe.wait_ge(rows_ready, 1)
                    for c in range(TT):
                        mm = pe.transpose(sbank[:, c // 4, (c % 4) * P:(c % 4 + 1) * P], yrow[:, c * P:(c + 1) * P], ident[:])
                    mm.then_inc(tk_tr, 1)
                if k == 9:
                    pe.wait_ge(tk_ready, 1)
                    pe.matmul(sbank[:, 2, 0:TT * NH], last[:], tk[:, :, 1, :], start=True, stop=True).then_inc(dc_done, 1)

            def attend(h, s):
                if s == 0 and isinstance(h, int) and h == 0:
                    pe.wait_ge(tk_done, 1)
                    pe.wait_ge(init_done, 3)
                if s in (0, 2):
                    c = s // 2
                    pe.wait_ge((v_in, mv_in)[c], 16 * h + 16)
                    if c == 0:
                        wait(pe, obt, 2 * h)
                    else:
                        pe.wait_ge(v_lo, 2 * h + 2)
                    for i, bank in enumerate((tr, ob)):
                        for j in range(4):
                            t = 4 * i + j
                            mm = pe.transpose(bank[:, j * P:(j + 1) * P], pr[:, c, t * P:(t + 1) * P], ident[:])
                        mm.then_inc(vtr, 1)
                def scores():
                    i = s - 3
                    if 0 <= i < TT:
                        if i == 0:
                            pe.wait_ge(qk_lo, 4 * h + 4)
                            pe.wait_ge(kb_in, 32 * h + 32)
                            wait(pe, nd_out, 3 * h)
                        else:
                            pe.wait_ge(exp_done, 2 * (TT * h + i))
                        width = (i + 1) * P if i % 4 == 2 else -(-(i + 1) // 2) * 2 * P
                        edges = [(0, width)] if width <= 512 else [(0, 512), (512, width)]
                        m0 = width - 2 * P
                        moff = 0 if width == (i + 1) * P else P
                        for c in range(2):
                            for lo, hi in edges:
                                diag = lo <= m0 < hi
                                q = qs[:, c, i * P:(i + 1) * P]
                                if diag:
                                    pe.matmul(sp_[:, c, m0:m0 + 2 * P], identr[:], mask[:, moff:moff + 2 * P],
                                              start=True, stop=False, skip_group_check=True)
                                pe.matmul(sp_[:, c, lo:hi], q, ka[:, c, lo:hi], start=not diag, stop=False,
                                          skip_group_check=True)
                                mm = pe.matmul(sp_[:, c, lo:hi], q, kb[:, c, lo:hi], start=False, stop=True,
                                               skip_group_check=True)
                            mm.then_inc(s_done, 1)

                def ml_products():
                    if s == 11:
                        pe.wait_ge(kq_ready, h + 1)
                        pe.wait_ge(qp_ready, h + 1)
                        pe.wait_ge(exp_done, 2 * TT * (h + 1))
                        for c in range(TT):
                            ch = slice(c * P, (c + 1) * P)
                            mm = pe.matmul(sp_[:, 0, ch], kqs[:, ch], qpad[:, ch], start=True, stop=True)
                        mm.then_inc(st_done, 1)
                        for c in range(TT):
                            ch = slice(c * P, (c + 1) * P)
                            mm = pe.transpose(sp_[:, 1, ch], kqs[:, ch], ident[:])
                        mm.then_inc(kt_done, 1)
                    if s == 12:
                        pe.wait_ge(kw_done, 2 * h + 2)
                        pe.wait_ge(pt_done, 2 * h + 2)
                        for c in range(TT - 1):
                            mm = pe.matmul(nd_at(c), ckw[:, c, :], v1[:, c, :], start=True, stop=True)
                        mm.then_inc(kv_done, 1)

                def weighted(part):
                    i = s - 5
                    if not 0 <= i < TT or (part and i < 4):
                        return
                    if part == 0:
                        if i >= 4:
                            pe.wait_ge(a_lo, 12 * h + tr_index(i, True))
                            for j in range(4, i + 1):
                                mm = pe.transpose(tr[:, (j - 4) * P:(j - 3) * P], at_late(i)[:, (j - 4) * P:(j - 3) * P], ident[:])
                            mm.then_inc(tr_done, 1)
                        else:
                            pe.wait_ge(a_lo, 12 * h + tr_index(i, False) + 1)
                        if i == 0:
                            pe.wait_ge(mv_out, 2 * h + 2)
                        else:
                            pe.wait_ge(o_add, TT * h + i)
                    else:
                        pe.wait_ge(a_lo, 12 * h + tr_index(i, True) + 1)
                    for j in range(4, i + 1) if part else range(min(4, i + 1)):
                        pe.matmul(ob[:, 0:2 * DV], ath[:, j, :], vs[:, j, :], start=(j == 0), stop=False)
                        mm = pe.matmul(ob[:, 0:2 * DV], atl[:, j, :], vs[:, j, :], start=False, stop=(j == i))
                    if part or i < 4:
                        mm.then_inc(pv_done, 1)

                def combined_transpose():
                    i = s - 4
                    if 0 <= i < TT:
                        pe.wait_ge(a_done, TT * h + i + 1)
                        if i == 0:
                            pe.wait_ge(mv_out, 2 * h + 2)
                        else:
                            pe.wait_ge(a_lo, 12 * h + tr_index(i, False))
                        for j in range(min(4, i + 1)):
                            mm = pe.transpose(tr[:, j * P:(j + 1) * P], at[:, j * P:(j + 1) * P], ident[:])
                        mm.then_inc(tr_done, 1)

                weighted(0)
                if s < 9:
                    combined_transpose()
                    scores()
                else:
                    scores()
                    ml_products()
                    weighted(1)
                    combined_transpose()
                if s == 13:
                    pe.wait_ge(c_done, h + 1)
                    pe.wait_ge(qi_ready, h + 1)
                    for c in range(TT):
                        ch = slice(c * P, (c + 1) * P)
                        mm = pe.matmul(nd_at(c), ee[:, ch], v1[:, c, :], start=True, stop=(c == 0))
                        if c:
                            mm = pe.matmul(nd_at(c), qpad[:, ch], cst[:, c, :], start=False, stop=True)
                    mm.then_inc(nd_done, 1)
                    pe.wait_ge(osc, h + 1)
                    for i, bank in enumerate((tr, ob)):
                        for j in range(4):
                            mm = pe.transpose(bank[:, j * P:(j + 1) * P], oo[:, 4 * i + j, :], ident[:])
                        mm.then_inc(ot_tr, 1)
                if s == 15:
                    pe.wait_ge(hm_ready, h + 1)
                    pe.wait_ge(ot_out, 2 * h + 2)
                    for i, bank in enumerate((tr, ob)):
                        for j in range(4):
                            mm = pe.transpose(bank[:, j * P:(j + 1) * P], nd[:, 4 * i + j, 0:DV], ident[:])
                        mm.then_inc(hm_tr, 1)

            def head_round(h, att):
                for s in range(SLOTS):
                    for part in range(8 * HB):
                        if QUARTER_AT[part] == s:
                            head_unit(h, part // 4, part % 4)
                    attend(att, s)

            head_round(1, 0)
            with pe.Fori(2, NH) as h:
                head_round(h, h - 1)
            for s in range(SLOTS):
                for k in GATE_UNITS_AT[s]:
                    unit(N_GATE + k // 2, k // 2 % 2, k % 2, r1h, r1l)
                attend(NH - 1, s)
            for k in range(24, 32):
                unit(N_GATE + k // 2, k // 2 % 2, k % 2, r1h, r1l)

            for b in range(KT):
                for i in range(2):
                    unit(N_PA + b, b % 2, i, r2h, r2l, before_k=(lambda k: pe.wait_ge(stg_lo, k + 1)) if b + i == 0 else None)
            for b in range(KT):
                for i in range(2):
                    if b + i == 0:
                        pe.wait_ge(stgb_lo, KT)
                    unit(N_PB + b, b % 2, i, r1h, r1l)
            for b in range(KT):
                for i in range(2):
                    unit(N_WO + b, b % 2, i, r2h, r2l,
                         before_k=(lambda k, i=i: pe.wait_ge(m_lo, 2 * k + i + 1)) if b == 0 else None)

            def ff1(g, first=False):
                n0 = g * (2 * KT) + N_FF
                for b in range(KT):
                    for i in range(2):
                        unit(n0 + b, b % 2, i, r1h, r1l,
                             before_k=(lambda k, i=i: pe.wait_ge(n_lo, 2 * k + i + 1)) if first and b == 0 else None)
                        if first and b + i == 0:
                            pe.wait_ge(sq_used, 2 * (KT - 1))
                            for c in range(2):
                                pe.matmul(sbank[:, c, :], ones[:], acc[:, c * HALF:(c + 1) * HALF],
                                          start=True, stop=True).then_inc(ss_done, 1)

            def own_unit(g, k, i):
                pe.wait_ge(u_lo, g * (2 * KT) + 2 * k + i + 1)

            def ff2(g):
                n0 = g * (2 * KT) + N_FF + KT
                for b in range(KT):
                    for i in range(2):
                        unit(n0 + b, b % 2, i, r2h, r2l,
                             before_k=(lambda k, i=i: own_unit(g, k, i)) if b == 0 else None)

            def out_banks(t):
                return gp if t == 6 else [sbank[:, 2 * (t % 2 if t < 6 else 0) + i, :] for i in range(2)]

            def out_transpose(t):
                if t >= 2 and t != 6:
                    pe.wait_ge(ft_out, 2 * (t - 2 if t < 6 else 4) + 2)
                if t == 6:
                    pe.wait_ge(gp_free, 2 * N_LAST + 4 * KT)
                for i in range(2):
                    for j in range(4):
                        k = 4 * i + j
                        mm = pe.transpose(out_banks(t)[i][:, j * P:(j + 1) * P], res[:, k, t * P:(t + 1) * P], ident[:])
                    mm.then_inc(ft_tr, 1)

            def out_sums(half):
                pe.wait_ge(sq_used, (half + 3) * (KT - 1))
                if half:
                    pe.wait_ge(f_var, 1)
                for t in range(4):
                    c = 4 * half + t
                    mm = pe.matmul(tr[:, 4 * c:4 * c + 4], acc[:, c * P:(c + 1) * P], ones[:, 0:4], start=True, stop=True)
                mm.then_inc(fs_done, 1)

            ff1(0, first=True)
            ff2(0)
            with pe.Fori(1, GROUPS - 1) as g:
                ff1(g)
                ff2(g)
            ff1(GROUPS - 1)
            for m in range(2 * KT):
                half, b = divmod(m, KT)
                unit(N_LAST + m, m % 2, m % 2, r2h, r2l, alone=half,
                     before_k=(lambda k, i=half: own_unit(GROUPS - 1, k, i)) if b == 0 else None)
                if half and b == 1:
                    out_sums(0)
                if half and 2 <= b < 6:
                    out_transpose(b - 2)
            pe.wait_ge(fin_done, 2 * KT)
            out_transpose(4)
            out_transpose(5)
            out_sums(1)
            out_transpose(6)
            out_transpose(7)

        @block.scalar
        def _(act):
            def split_hi(n, half_n, slot):
                act.wait_ge(w_loaded[slot], 16 * half_n + 16)
                wait(act, gemm_done, 2 * n - 2)
                act.activation(wh[slot][:], raw[slot][:], ACT.Copy).then_inc(w_hi, 1)

            def evac(n, half):
                wait(act, st[half], 16 * n)
                act.wait_ge(gemm_done, 2 * n + half + 1)
                act.activation(ev[half][:], gp[half][:], ACT.Copy).then_inc(gp_free, 1)
                act.wait_ge(gp_free, 2 * n + half + 1)
                act.sem_inc(ev_ready[half], 1)

            act.wait_ge(init_done, 1)
            act.activation(rstd0[:, 0:1], ones[:, 0:1], ACT.Sqrt)
            act.dma_start(wif[:], w_in2.rearrange("(k p) n -> p k n", p=P)[:, :, OFF_I:OFF_I + 16], allow_slow_non_contiguous=True).then_inc(wif_in, 16)
            act.dma_start(gb[0:NH, :], ml_gate_b[0, 0:NH].rearrange("(p a) -> p a", a=1), allow_slow_non_contiguous=True).then_inc(c_in, 16)
            act.dma_start(gb[32:32 + NH, :], ml_gate_b[0, NH:2 * NH].rearrange("(p a) -> p a", a=1), allow_slow_non_contiguous=True).then_inc(c_in, 16)
            act.dma_start(lamt[:], da_lambda[0].rearrange("a b -> (a b)").partition_broadcast(P), allow_slow_non_contiguous=True).then_inc(c_in, 16)
            act.dma_start(carry[:], c_carry, allow_slow_non_contiguous=True).then_inc(c_in, 16)
            act.dma_start(last[:], c_last, allow_slow_non_contiguous=True).then_inc(c_in, 16)

            for t in range(TT + 2):
                if t < TT:
                    act.wait_ge(x_in[t % XB], 16 * (t // XB + 1))
                    wait(act, ss_ready, t)
                    act.activation(sp_[:, 1, :], xtok[t % XB][:], ACT.Square, accum_out=ss[:, t:t + 1]).then_inc(ss_ready, 1)
                if 1 <= t <= TT:
                    act.wait_ge(x_var, t)
                    act.activation(rstd0[:, t - 1:t], rstd0[:, t - 1:t], ACT.Sqrt).then_inc(x_std, 1)
                if t >= 2:
                    for i in range(2):
                        act.wait_ge(x_tr, 2 * (t - 2) + i + 1)
                        act.activation(r1h[:, 4 * i:4 * i + 4, (t - 2) * P:(t - 1) * P],
                                       (tr, ob)[i][:].rearrange("p (k n) -> p k n", k=4), ACT.Copy).then_inc(x_hi, 1)
                if t == 3:
                    act.wait_ge(wif_in, 16)
                    act.wait_ge(wif_set, 2)
                    act.activation(wifh[:, :, 0:NH], wif[:, :, 0:NH], ACT.Copy).then_inc(wif_h, 1)
                    act.activation(wifh[:, :, 32:32 + NH], wif[:, :, NH:2 * NH], ACT.Copy).then_inc(wif_h, 1)
                if t == 6:
                    split_hi(0, 0, 0)
            act.dma_start(nw[:, 0, :], norm_ffn_w[0].rearrange("(k p) -> p k", p=P), allow_slow_non_contiguous=True).then_inc(c_in, 16)
            act.dma_start(nw[:, 1, :], final_norm_w.rearrange("(k p) -> p k", p=P), allow_slow_non_contiguous=True).then_inc(c_in, 16)
            act.dma_start(aw[:], da_subln_w[0].rearrange("(p a) -> p a", a=1), allow_slow_non_contiguous=True).then_inc(c_in, 16)
            act.dma_start(mlw[:], ml_norm_w[0].rearrange("(h p) -> p h", p=P), allow_slow_non_contiguous=True).then_inc(c_in, 16)
            for j in range(CONV + 1):
                src = conv_w[0, j] if j < CONV else conv_b[0]
                act.dma_start(cw[0:DK, j, :], src[NH * DK:].rearrange("(h p) -> p h", p=DK), allow_slow_non_contiguous=True).then_inc(c_in, 16)
                act.dma_start(cw[DK:P, j, :], src[0:NH * DK].rearrange("(h p) -> p h", p=DK), allow_slow_non_contiguous=True).then_inc(c_in, 16)

            def xt_evac(t):
                wait(act, xt_st[t % 2], 16 * (t // 2))
                for i in range(2):
                    act.wait_ge(x_tr, 2 * (TT + t) + i + 1)
                    act.activation(xTs[t % 2][:, 4 * i:4 * i + 4, :], (tr, ob)[i][:].rearrange("p (k n) -> p k n", k=4),
                                   ACT.Copy).then_inc(xts_out, 1)

            def prologue_step(k):
                if k == 2:
                    for i, tab in enumerate((sinT, cosT)):
                        act.wait_ge(ang_ready, i + 1)
                        act.activation(tab[:], tab[:], ACT.Sin).then_inc(tab_ready, 1)
                if k == 4:
                    act.wait_ge(nf_ready, 1)
                    act.activation(erow[:], erow[:], ACT.Exp).then_inc(pact, 1)
                    act.wait_ge(pact, 1)
                    act.activation(erow[:], erow[:], ACT.Ln, bias=1.0).then_inc(ln_ready, 1)
                    act.wait_ge(lam_ready, 1)
                    act.activation(lams[:, 2:4], lams[:, 0:2], ACT.Exp).then_inc(lam_exp, 1)
                if k == 6:
                    act.wait_ge(rows_ready, 1)
                    act.activation(wrow[:], yrow[32:32 + NH, :], ACT.Exp).then_inc(wrow_ready, 1)
                if k == 8:
                    act.wait_ge(tk_tr, 1)
                    src = sbank[:, 0:2, :].rearrange("p b (c q r) -> p (b c) q r", c=4, q=4)[:, :, :, 0:NH]
                    for q in range(4):
                        act.activation(tk[:, :, q, :], src[:, :, q, :], ACT.Copy if q == 0 else ACT.Exp).then_inc(
                            tk_ready if q == 3 else pact, 1)
                if k == 10:
                    act.wait_ge(dc_done, 1)
                    act.activation(dc[:], sbank[:, 2, 0:TT * NH].rearrange("p (c h) -> p c h", c=TT), ACT.Copy).then_inc(tk_done, 1)
                    act.wait_ge(tk_done, 1)

            def units_of_round(h, k):
                if k % 2 == 0:
                    b = k // 2
                    split_hi(h * HB + b + 1, h * (HB // 2) + (b + 1) // 2, (b + 1) % 2)

            def kq_wait(h, b):
                if b + 1 == 3:
                    act.wait_ge(w_loaded_q, 16 * h + 16)

            for k in range(2 * HB):
                kq_wait(0, k // 2)
                units_of_round(0, k)
                evac(k // 2, k % 2)
                prologue_step(k)
                if X_RAW <= k < X_RAW + TT:
                    xt_evac(k - X_RAW)

            def attend(h, s, evac_units):
                def v_part(i):
                    act.wait_ge(vtr, 4 * h + 1 + i)
                    src = (tr, ob)[i][:].rearrange("p (t n) -> p t n", t=4)
                    act.activation(vs[:, 4 * i:4 * i + 4, 0:DV], src, ACT.Copy).then_inc(v_hi, 1)

                if s == 0:
                    for c, (x_, to) in enumerate(((kraw, ka), (qraw, qs))):
                        act.wait_ge(roped, 2 * h + c + 1)
                        act.activation(to[0:DK, 0, :], x_[0:DK, :], ACT.Copy).then_inc(qk_hi, 1)
                        act.activation(to[DK:P, 1, :], x_[DK:P, :], ACT.Copy).then_inc(qk_hi, 1)
                        if c == 0:
                            evac_units()
                            act.wait_ge(qk_lo, 4 * h + 2)
                            act.dma_start(kb[0:DK, :, :].bitcast(F32), ka[DK:P, :, :].bitcast(F32)).then_inc(kb_in, 16)
                            act.dma_start(kb[DK:P, :, :].bitcast(F32), ka[0:DK, :, :].bitcast(F32)).then_inc(kb_in, 16)
                    v_part(0)
                    v_part(1)
                if s == 2:
                    for i in range(2):
                        act.wait_ge(vtr, 4 * h + 3 + i)
                        src = (tr, ob)[i][:].rearrange("p (t n) -> p t n", t=4)
                        act.activation(v1[:, 4 * i:4 * i + 4, 0:DV], src, ACT.Copy).then_inc(mv_out, 1)
                    act.activation(warm[:], neglam[:], ACT.Exp)
                def high(i, second):
                    act.wait_ge(tr_done, 12 * h + tr_index(i, second) + 1)
                    if not second:
                        wait(act, pv_done, TT * h + i)
                    j0, j1 = (4, i + 1) if second else (0, min(4, i + 1))
                    act.activation(ath[:, j0:j1, :], tr[:, 0:(j1 - j0) * P].rearrange("p (j n) -> p j n", n=P),
                                   ACT.Copy).then_inc(a_hi, 1)

                i = s - 5
                if 0 <= i < TT:
                    if i >= 4:
                        high(i, True)
                    act.wait_ge(pv_done, TT * h + i + 1)
                    wait(act, sso_done, TT * h + i)
                    act.activation(otmp[:], ob[:, DV:2 * DV], ACT.Copy).then_inc(o_right, 1)
                if 0 <= s - 4 < TT:
                    high(s - 4, False)
                i = s - 5
                if 0 <= i < TT:
                    act.wait_ge(o_add, TT * h + i + 1)
                    act.activation(otmp[:], oo[:, i, :], ACT.Square, accum_out=sso[:, i:i + 1]).then_inc(sso_done, 1)
                i = s - 3
                if 0 <= i < TT:
                    act.wait_ge(nb_ready, TT * h + i + 1)
                    wait(act, a_done, TT * h + i)
                    for c in range(2):
                        act.activation(pr[:, c, 0:(i + 1) * P], sp_[:, c, 0:(i + 1) * P], ACT.Exp, bias=nb[:, c:c + 1],
                                       scale=SCALE, accum_out=rs[:, i, c:c + 1]).then_inc(exp_done, 1)
                if s in (5, 6):
                    if s == 5:
                        act.wait_ge(u_in, 16 * h + 16)
                        act.wait_ge(hk_ready, 4 * h + 4)
                    for c in range(4 * (s - 5), 4 * (s - 5) + 4):
                        ch = slice(c * P, (c + 1) * P)
                        act.activation(ee[:, ch], ee[:, ch], ACT.Exp, bias=hk[:, c, 0:1]).then_inc(e_exp, 1)
                if s == 7:
                    act.wait_ge(conv_done, h + 1)
                    act.activation(sg[:], kqs[:], ACT.Sigmoid).then_inc(sg_ready, 1)
                    act.wait_ge(o_in, 16 * h + 16)
                    act.activation(osig[:], osig[:], ACT.Sigmoid).then_inc(os_ready, 1)
                if s == 9:
                    act.wait_ge(kq_ready, h + 1)
                    act.activation(qpad[0:DK, :], kqs[DK:P, :], ACT.Copy, scale=SCALE).then_inc(qp_ready, 1)
                if s == 12:
                    act.wait_ge(varo, h + 1)
                    act.activation(t8[:], t8[:], ACT.Sqrt).then_inc(stdo, 1)
                if s == 13:
                    act.wait_ge(nd_done, h + 1)
                    for b in range(3):
                        n = min(3, TT - 3 * b)
                        act.activation(nd[:, 3 * b:3 * b + n, :], sbank[:, b, 0:n * VW].rearrange("p (c n) -> p c n", n=VW),
                                       ACT.Copy).then_inc(nd_out, 1)
                    act.wait_ge(nd_out, 3 * h + 3)
                    for c in range(TT):
                        act.activation(sqj[:], nd[:, c, 0:DV], ACT.Square, accum_out=ssm[:, c:c + 1]).then_inc(ssm_done, 1)
                        act.wait_ge(ssm_done, TT * h + c + 1)
                    act.wait_ge(varm, h + 1)
                    act.activation(d2[:], d2[:], ACT.Sqrt).then_inc(stdm, 1)
                    for i in range(2):
                        act.wait_ge(ot_tr, 2 * h + i + 1)
                        act.activation(at[:, i * HALF:(i + 1) * HALF], (tr, ob)[i][:], ACT.Copy, scale=aw[:, 0:1]).then_inc(ot_out, 1)
                    act.wait_ge(ot_out, 2 * h + 2)
                    act.dma_start(oa_d[bass.ds(h, 1)].rearrange("a p n -> (a p) n"), at[:]).then_inc(oa_st, 16)
                if s == 15:
                    act.wait_ge(obt, 2 * h + 2)
                    act.dma_start(ob_d[bass.ds(h, 1)].rearrange("a p n -> (a p) n"), osig[:]).then_inc(ob_st, 16)

            def head_round(h, att):
                for s in range(SLOTS):
                    for k in STARTS_AT[s]:
                        if k % 2 == 0:
                            kq_wait(h, k // 2)
                            units_of_round(h, k)
                    for k in ENDS_AT[s][:-1]:
                        evac(h * HB + k // 2, k % 2)

                    def evac_units():
                        for k in ENDS_AT[s][-1:]:
                            evac(h * HB + k // 2, k % 2)

                    attend(att, s, evac_units)
                    if s:
                        evac_units()

            head_round(1, 0)
            with act.Fori(2, NH) as h:
                head_round(h, h - 1)
            for s in range(SLOTS):
                for k in GATE_UNITS_AT[s]:
                    n = N_GATE + k // 2
                    if k % 2 == 0:
                        split_hi(n + 1, (n + 1) // 2, (n + 1) % 2)
                for k in GATE_UNITS_AT[s][:-1]:
                    evac(N_GATE + k // 2, k % 2)

                def evac_units():
                    for k in GATE_UNITS_AT[s][-1:]:
                        evac(N_GATE + k // 2, k % 2)

                attend(NH - 1, s, evac_units)
                if s:
                    evac_units()

            def square(stage, k, half, src):
                if stage == 0:
                    wait(act, sq_used, 2 * (k - 2) + half + 1 if k >= 2 else 0)
                elif k:
                    act.wait_ge(sq_used, (half + 2) * (KT - 1) + max(k - 2, 0))
                i = half if stage == 0 else k % 2
                to = ut[i][:] if k else acc[:, half * HALF:(half + 1) * HALF]
                act.activation(to, src, ACT.Square).then_inc(sq_ready, 1)

            def stage_hi(k, to):
                act.wait_ge(stg_in[k % 2], 16 * (k // 2 + 1))
                act.activation(to[:, k % KT, :], stg[k % 2][:], ACT.Copy).then_inc(stg_hi, 1)

            for j in range(12, 16):
                n = N_GATE + j
                split_hi(n + 1, (n + 1) // 2, (n + 1) % 2)
                for i in range(2):
                    evac(n, i)
                    for k in STAGE_AT.get(j, ())[i:i + 1]:
                        stage_hi(k, r2h)
            for j in range(2 * KT):
                n = N_PA + j
                split_hi(n + 1, (n + 1) // 2, (n + 1) % 2)
                for i in range(2):
                    act.wait_ge(g_in[i], 16 * j + 16)
                    act.activation(gt[i][:], gt[i][:], ACT.Sigmoid).then_inc(g_sig, 1)
                if j < KT:
                    stage_hi(KT + j, r1h)
                else:
                    for i in range(2):
                        k = j - KT
                        act.wait_ge(m_sum, 2 * k + i + 1)
                        act.activation(r2h[:, k, i * HALF:(i + 1) * HALF], ev[i][:], ACT.Copy).then_inc(m_hi, 1)
            for k in range(KT):
                n = N_WO + k
                split_hi(n + 1, (n + 1) // 2, (n + 1) % 2)
                for i in range(2):
                    act.wait_ge(res_done, 2 * k + i + 1)
                    r = res[:, k, i * HALF:(i + 1) * HALF]
                    act.activation(r1h[:, k, i * HALF:(i + 1) * HALF], r, ACT.Copy, scale=nw[:, 0, k:k + 1]).then_inc(n_hi, 1)
                    square(0, k, i, r)
            def ff1(g, first=False):
                for b in range(KT):
                    n = g * (2 * KT) + N_FF + b
                    split_hi(n + 1, g * KT + N_FF // 2 + (b + 1) // 2, (b + 1) % 2)
                    for i in range(2 if first and b == 0 else 0):
                        act.wait_ge(var_ready, i + 1)
                        r = rstd1[:, i * HALF:(i + 1) * HALF]
                        act.activation(r, r, ACT.Sqrt).then_inc(std_ready, 1)
                    for i in range(2):
                        u = g * (2 * KT) + 2 * b + i
                        act.wait_ge(z_ready, u + 1)
                        act.activation(ut[i][:], ev[i][:], ACT.Square).then_inc(u_ready, 1)
                        act.wait_ge(u_ready, u + 1)
                        act.activation(r2h[:, b, i * HALF:(i + 1) * HALF], ut[i][:], ACT.Copy).then_inc(u_hi, 1)

            def ff2(g):
                for b in range(KT, 2 * KT):
                    n = g * (2 * KT) + N_FF + b
                    split_hi(n + 1, g * KT + N_FF // 2 + (b + 1) // 2, (b + 1) % 2)

            ff1(0, first=True)
            ff2(0)
            with act.Fori(1, GROUPS - 1) as g:
                ff1(g)
                ff2(g)
            ff1(GROUPS - 1)

            def out_root(half):
                act.wait_ge(f_var, half + 1)
                r = rfin[:, 4 * half:4 * half + 4]
                act.activation(r, r, ACT.Sqrt).then_inc(f_std, 1)

            for m in range(2 * KT):
                half, k = divmod(m, KT)
                n = N_LAST + m
                if m < 2 * KT - 1:
                    split_hi(n + 1, (n + 1) // 2, (n + 1) % 2)
                act.wait_ge(fin_done, m + 1)
                square(1, k, half, res[:, k, half * HALF:(half + 1) * HALF])
                if half and k == 1:
                    out_root(0)
            out_root(1)

        @block.vector
        def _(dve):
            pro = Chain(dve, pdv)
            ones_like = dve.memset(ones[:], 1.0)
            ones_like.then_inc(init_done, 1)
            for t in range(TT + 2):
                if t < TT:
                    dve.wait_ge(ss_ready, t + 1)
                    dve.tensor_scalar(rstd0[:, t:t + 1], ss[:, t:t + 1], 1.0 / D, EPS, ALU.mult, ALU.add).then_inc(x_var, 1)
                if 1 <= t <= TT:
                    r = rstd0[:, t - 1:t]
                    dve.wait_ge(x_std, t)
                    dve.reciprocal(r, r).then_inc(x_rstd, 1)
                    dve.wait_ge(x_rstd, t)
                    if t == 1:
                        dve.wait_ge(nwb_in, 16)
                    xt = xtok[(t - 1) % XB]
                    dve.scalar_tensor_tensor(xt[:], xt[:], r, nwb[:], ALU.mult, ALU.mult).then_inc(x_scaled, 1)
                if t >= 2:
                    for i in range(2):
                        ch = slice((t - 2) * P, (t - 1) * P)
                        dve.wait_ge(x_hi, 2 * (t - 2) + i + 1)
                        dve.tensor_tensor(r1l[:, 4 * i:4 * i + 4, ch], (tr, ob)[i][:].rearrange("p (k n) -> p k n", k=4),
                                          r1h[:, 4 * i:4 * i + 4, ch].bitcast(F32), ALU.subtract).then_inc(x_lo, 1)

            dve.memset(ckq[:, 0:CONV - 1], 0.0)
            dve.memset(qpad[DK:P, :], 0.0)
            dve.memset(sg[:, 3 * P:], 0.0)
            dve.memset(cst[:], 0.0)
            pro.link(dve.memset(v1[:, :, DV:DV + 1], 1.0))
            pro.link(dve.memset(v1[:, :, DV + 1:VW], 0.0))
            two_pi = (6.28125, 0.0019350051879882812, 3.0197994998e-07)
            dve.wait_ge(c2_in, 16 * 4)
            dve.tensor_copy(identr[:], ident[:])
            pro.link(dve.tensor_copy(mask[:], sg[:, 0:3 * P]))
            pro.link(dve.tensor_copy(kqs[:], cosT[:].bitcast(I32)))
            ang = kqs[:]
            pro.link(dve.tensor_scalar(ang, ang, inv[:, 0:1], None, ALU.mult))
            for tab, turns, shift in ((sinT, cosT[:], 0.0), (cosT, sg[:], 0.25)):
                pro.link(dve.tensor_scalar(turns, ang, 1.0 / (2 * np.pi), shift, ALU.mult, ALU.add))
                pro.link(dve.tensor_scalar(turns, turns, 12582912.0, -12582912.0, ALU.add, ALU.add))
                src = ang
                for part in two_pi:
                    pro.link(dve.scalar_tensor_tensor(tab[:], turns, -part, src, ALU.mult, ALU.add))
                    src = tab[:]
                pro.link(dve.tensor_scalar(tab[:], tab[:], shift * 2 * np.pi, 3.1415925, ALU.add, ALU.min))
                dve.tensor_scalar(tab[:], tab[:], -3.1415925, None, ALU.max).then_inc(ang_ready, 1)
            dve.wait_ge(c_in, 16 * 19)
            lv = lamt[:].rearrange("p (a b n) -> p a b n", a=2, b=2)
            pro.link(dve.tensor_tensor(lv[:, :, 0, :], lv[:, :, 0, :], lv[:, :, 1, :], ALU.mult))
            dve.tensor_reduce(lams[:, 0:2], lv[:, :, 0, :], AX_X, ALU.add).then_inc(lam_ready, 1)
            pro.link(dve.tensor_scalar(aw[:], aw[:], 1.0 - LAMBDA_INIT, None, ALU.mult))
            for i in range(2):
                t = slice(i * HALF, (i + 1) * HALF)
                dve.wait_ge(if_done, i + 1)
                dve.tensor_scalar(ga[0:NH, t], sbank[0:NH, i, :], gb[0:NH, 0:1], None, ALU.add)
                pro.link(dve.tensor_scalar(ga[32:32 + NH, t], sbank[32:32 + NH, i, :], gb[32:32 + NH, 0:1], None, ALU.add))
            dve.tensor_copy(irow[:], ga[0:NH, :])
            pro.link(dve.tensor_copy(frow[:], ga[32:32 + NH, :]))
            dve.scalar_tensor_tensor(erow[:], frow[:], -1.0, frow[:], ALU.mult, ALU.min).then_inc(nf_ready, 1)
            dve.wait_ge(ln_ready, 1)
            pro.link(dve.scalar_tensor_tensor(frow[:], frow[:], 0.0, erow[:], ALU.min, ALU.subtract))
            dve.tensor_tensor_scan(mrow[:], frow[:], irow[:], 0.0, ALU.add, ALU.max)
            pro.link(dve.tensor_tensor_scan(brow[:], carry[:], frow[:], 0.0, ALU.mult, ALU.add))
            pro.link(dve.memset(yrow[:], 0.0))
            c3 = lambda r: r[:].rearrange("p (c n) -> p c n", c=TT)
            y3 = yrow[:].rearrange("p (c n) -> p c n", c=TT)
            pro.link(dve.tensor_tensor(urow[:], brow[:], mrow[:], ALU.subtract))
            pro.link(dve.tensor_tensor(irow[:], irow[:], brow[:], ALU.subtract))
            pro.link(dve.memset(mprev[:, 0:1], 0.0))
            pro.link(dve.tensor_copy(mprev[:, 1:TT], c3(mrow)[:, 0:TT - 1, P - 1]))
            dve.tensor_copy(yrow[0:NH, :], irow[:])
            dve.tensor_tensor(y3[32:32 + NH], c3(urow), mprev[:, :].unsqueeze(2).broadcast_to([NH, TT, P]), ALU.add)
            dve.tensor_tensor(y3[64:64 + NH], c3(irow), c3(urow)[:, :, P - 1:P].broadcast_to([NH, TT, P]), ALU.add)
            dve.tensor_scalar(yrow[96:96 + NH, :], mrow[:], -1.0, None, ALU.mult).then_inc(rows_ready, 1)
            dve.wait_ge(lam_exp, 1)
            pro.link(dve.tensor_tensor(lams[:, 0:1], lams[:, 3:4], lams[:, 2:3], ALU.subtract))
            pro.link(dve.tensor_scalar(neglam[:], lams[:, 0:1], -LAMBDA_INIT, None, ALU.add))
            dve.wait_ge(tk_done, 1)
            dve.wait_ge(uw_st, 32)
            for i in range(2):
                dve.wait_ge(xt_st[i], 16 * (TT // 2))
            dve.wait_ge(tab_ready, 2)
            dve.sem_inc(init_done, 2)

            chain = Chain(dve, dve_chain)

            def attend(h, s):
                if s == 0:
                    chain.start(h * DVE_HEAD)
                    def low_parts(c, x_, to):
                        dve.wait_ge(qk_hi, 4 * h + 2 * c + 2)
                        dve.tensor_tensor(to[DK:P, 0, :], x_[0:DK, :], to[0:DK, 0, :].bitcast(F32), ALU.subtract).then_inc(qk_lo, 1)
                        dve.tensor_tensor(to[0:DK, 1, :], x_[DK:P, :], to[DK:P, 1, :].bitcast(F32), ALU.subtract).then_inc(qk_lo, 1)

                    for x_, turned, s_in in ((kraw, kqs, k_in), (qraw, sg, q_in)):
                        dve.wait_ge(s_in, 16 * 5 * (h + 1))
                        dve.tensor_tensor(turned[:], turned[:], sinT[:], ALU.mult)
                        chain.link(dve.tensor_tensor(x_[:], x_[:], cosT[:], ALU.mult))
                        if x_ is qraw:
                            low_parts(0, kraw, ka)
                        dve.tensor_tensor(x_[:], x_[:], turned[:], ALU.add).then_inc(roped, 1)
                    low_parts(1, qraw, qs)
                    for i in range(2):
                        dve.wait_ge(v_hi, 2 * h + i + 1)
                        src = (tr, ob)[i][:].rearrange("p (t n) -> p t n", t=4)
                        dve.tensor_tensor(vs[:, 4 * i:4 * i + 4, DV:2 * DV], src, vs[:, 4 * i:4 * i + 4, 0:DV].bitcast(F32),
                                          ALU.subtract).then_inc(v_lo, 1)
                def low(i, second):
                    dve.wait_ge(a_hi, 12 * h + tr_index(i, second) + 1)
                    j0, j1 = (4, i + 1) if second else (0, min(4, i + 1))
                    dve.tensor_tensor(atl[:, j0:j1, :], tr[:, 0:(j1 - j0) * P].rearrange("p (j n) -> p j n", n=P),
                                      ath[:, j0:j1, :].bitcast(F32), ALU.subtract).then_inc(a_lo, 1)

                i = s - 5
                if 0 <= i < TT:
                    if i >= 4:
                        low(i, True)
                    dve.wait_ge(o_right, TT * h + i + 1)
                    dve.tensor_tensor(oo[:, i, :], ob[:, 0:DV], otmp[:], ALU.add).then_inc(o_add, 1)

                if 0 <= s - 4 < TT:
                    low(s - 4, False)
                i = s - 3
                if 0 <= i < TT:
                    for c in range(2):
                        dve.wait_ge(s_done, 2 * (TT * h + i) + c + 1)
                        m = dve.tensor_reduce(mx[:, c:c + 1], sp_[:, c, 0:(i + 1) * P], AX_X, ALU.max)
                    chain.link(m)
                    dve.tensor_scalar(nb[:], mx[:], -SCALE, None, ALU.mult).then_inc(nb_ready, 1)
                if 0 <= i < TT:
                    if i == 0:
                        wait(dve, oa_st, 16 * h)
                    dve.wait_ge(exp_done, 2 * (TT * h + i) + 2)
                    chain.link(dve.reciprocal(rr[:, i, :], rs[:, i, :]))
                    chain.link(dve.tensor_scalar(cc[:], rs[:, i, 0:1], rr[:, i, 1:2], neglam[:, 0:1], ALU.mult, ALU.mult))
                    if i:
                        dve.wait_ge(tr_done, 12 * h + tr_index(i - 1, False) + 1)
                    n = min(HALF, (i + 1) * P)
                    m = dve.scalar_tensor_tensor(at[:, 0:n], pr[:, 1, 0:n], cc[:, 0:1], pr[:, 0, 0:n], ALU.mult, ALU.add)
                    if i >= 4:
                        if i >= 6:
                            dve.wait_ge(tr_done, 12 * h + tr_index(i - 2, True) + 1)
                        late = slice(HALF, (i + 1) * P)
                        m = dve.scalar_tensor_tensor(at_late(i)[:, 0:(i - 3) * P], pr[:, 1, late], cc[:, 0:1],
                                                     pr[:, 0, late], ALU.mult, ALU.add)
                    m.then_inc(a_done, 1)
                if s == 3:
                    dve.wait_ge(kq_in, 16 * h + 16)
                    dve.wait_ge(hk_ready, 4 * h + 4)
                if 3 <= s < 3 + CONV:
                    j = CONV - 1 - (s - 3)
                    src = ckq[:, j:j + S]
                    if s == 3:
                        m = dve.tensor_scalar(kqs[:], src, hc[:, j:j + 1], hc[:, CONV:CONV + 1], ALU.mult, ALU.add)
                    else:
                        m = dve.scalar_tensor_tensor(kqs[:], src, hc[:, j:j + 1], kqs[:], ALU.mult, ALU.add)
                    if j == 0:
                        m.then_inc(conv_done, 1)
                    else:
                        chain.link(m)
                if s == 7:
                    dve.wait_ge(e_exp, TT * h + TT)
                    e3 = ee[:].rearrange("p (c n) -> p c n", c=TT)
                    dve.tensor_tensor(e3, e3, keep[:, :].unsqueeze(1).broadcast_to([P, TT, P]), ALU.min).then_inc(e_sel, 1)
                if s == 11:
                    dve.wait_ge(st_done, h + 1)
                    dve.wait_ge(e_sel, h + 1)
                    for i in range(2):
                        t = slice(i * HALF, (i + 1) * HALF)
                        dve.tensor_tensor(ee[:, t], sp_[:, 0, t], ee[:, t], ALU.mult).then_inc(pt_done, 1)
                    dve.wait_ge(kt_done, h + 1)
                    for i in range(2):
                        t = slice(4 * i, 4 * i + 4)
                        dve.tensor_tensor(ckw[:, t, :], sbank[:, 2 + i, :].rearrange("p (c n) -> p c n", c=4),
                                          hk[:, t, 2:3].broadcast_to([P, 4, P]), ALU.mult).then_inc(kw_done, 1)
                if s == 12:
                    dve.wait_ge(kv_done, h + 1)
                    chain.link(dve.tensor_copy(cst[0:DK, 1, :], nd_at(0)[0:DK]))
                    for c in range(1, TT - 1):
                        m = dve.scalar_tensor_tensor(cst[0:DK, c + 1, :], cst[0:DK, c, :], hd[0:DK, c:c + 1],
                                                     nd_at(c)[0:DK], ALU.mult, ALU.add)
                        if c < TT - 2:
                            chain.link(m)
                    m.then_inc(c_done, 1)
                    r0 = rr[:, :, 0]
                    dve.wait_ge(sso_done, TT * h + TT)
                    chain.link(dve.tensor_tensor(t8[:], r0, r0, ALU.mult))
                    chain.link(dve.tensor_tensor(t8[:], t8[:], sso[:], ALU.mult))
                    dve.tensor_scalar(t8[:], t8[:], 1.0 / DV, EPS, ALU.mult, ALU.add).then_inc(varo, 1)
                    dve.wait_ge(stdo, h + 1)
                    chain.link(dve.reciprocal(rsc[:], t8[:]))
                    chain.link(dve.tensor_tensor(rsc[:], rsc[:], r0, ALU.mult))
                    dve.tensor_tensor(oo[:], oo[:], rsc[:].unsqueeze(2).broadcast_to([P, TT, DV]), ALU.mult).then_inc(osc, 1)
                if s == 14:
                    dve.wait_ge(nd_out, 3 * h + 3)
                    den = nd[:, :, DV]
                    chain.link(dve.scalar_tensor_tensor(d1[:], den, -1.0, den, ALU.mult, ALU.max))
                    chain.link(dve.tensor_tensor(d1[:], d1[:], hk[:, :, 3], ALU.max))
                    chain.link(dve.reciprocal(rm[:], d1[:]))
                    chain.link(dve.tensor_tensor(d2[:], rm[:], rm[:], ALU.mult))
                    dve.wait_ge(ssm_done, TT * h + TT)
                    chain.link(dve.tensor_tensor(d2[:], d2[:], ssm[:], ALU.mult))
                    dve.tensor_scalar(d2[:], d2[:], 1.0 / DV, EPS, ALU.mult, ALU.add).then_inc(varm, 1)
                    dve.wait_ge(stdm, h + 1)
                    chain.link(dve.reciprocal(d1[:], d2[:]))
                    chain.link(dve.tensor_tensor(rm[:], rm[:], d1[:], ALU.mult))
                    dve.tensor_tensor(nd[:, :, 0:DV], nd[:, :, 0:DV], rm[:].unsqueeze(2).broadcast_to([P, TT, DV]),
                                      ALU.mult).then_inc(hm_ready, 1)
                if s == 15:
                    dve.wait_ge(os_ready, h + 1)
                    for i in range(2):
                        t = slice(i * HALF, (i + 1) * HALF)
                        dve.wait_ge(hm_tr, 2 * h + i + 1)
                        dve.scalar_tensor_tensor(osig[:, t], (tr, ob)[i][:], hw[:, 0:1], osig[:, t], ALU.mult,
                                                 ALU.mult).then_inc(obt, 1)
                    assert chain.count == DVE_HEAD, chain.count

            for s in range(SLOTS):
                attend(0, s)
            with dve.Fori(1, NH) as h:
                for s in range(SLOTS):
                    attend(h, s)

            for k in range(KT):
                dve.wait_ge(stg_hi, k + 1)
                dve.tensor_tensor(r2l[:, k, :], stg[k % 2][:], r2h[:, k, :].bitcast(F32), ALU.subtract).then_inc(stg_lo, 1)
            for j in range(2 * KT):
                n = N_PA + j
                for i in range(2):
                    k = j % KT
                    t = slice(i * HALF, (i + 1) * HALF)
                    dve.wait_ge(gemm_done, 2 * n + i + 1)
                    dve.wait_ge(g_sig, 2 * j + i + 1)
                    if j == 0 and i == 0:
                        dve.wait_ge(ob_st, 16 * NH)
                    if j < KT:
                        dve.tensor_tensor(res[:, k, t], gp[i][:], gt[i][:], ALU.mult).then_inc(gp_free, 1)
                        dve.wait_ge(gp_free, 2 * n + i + 1)
                        dve.sem_inc(g_used, 1)
                    else:
                        if j == KT:
                            dve.wait_ge(st[i], 16 * N_PA)
                        dve.tensor_tensor(gt[i][:], gp[i][:], gt[i][:], ALU.mult).then_inc(gp_free, 1)
                        dve.wait_ge(gp_free, 2 * n + i + 1)
                        wait(dve, m_lo, 2 * k + i - 1)
                        dve.tensor_tensor(ev[i][:], gt[i][:], res[:, k, t], ALU.add).then_inc(m_sum, 1)
                        dve.wait_ge(m_sum, 2 * k + i + 1)
                        dve.sem_inc(g_used, 1)
            for k in range(KT):
                for i in range(2):
                    t = slice(i * HALF, (i + 1) * HALF)
                    n = N_WO + k
                    dve.wait_ge(gemm_done, 2 * n + i + 1)
                    dve.wait_ge(res_in, 16 * KT)
                    dve.tensor_tensor(res[:, k, t], gp[i][:], res[:, k, t], ALU.add).then_inc(gp_free, 1)
                    dve.wait_ge(gp_free, 2 * n + i + 1)
                    dve.sem_inc(res_done, 1)
                    dve.wait_ge(n_hi, 2 * k + i + 1)
                    dve.scalar_tensor_tensor(r1l[:, k, t], res[:, k, t], nw[:, 0, k:k + 1], r1h[:, k, t].bitcast(F32),
                                             ALU.mult, ALU.subtract).then_inc(n_lo, 1)
            for i in range(2):
                dve.wait_ge(ss_done, i + 1)
                dve.tensor_scalar(rstd1[:, i * HALF:(i + 1) * HALF], sbank[:, i, :], 1.0 / D, EPS, ALU.mult, ALU.add).then_inc(var_ready, 1)

            def norm_factor(i):
                r = rstd1[:, i * HALF:(i + 1) * HALF]
                dve.wait_ge(std_ready, i + 1)
                dve.reciprocal(r, r).then_inc(rstd_ready, 1)
                dve.wait_ge(rstd_ready, i + 1)

            norm_factor(0)

            def ff1(g, first=False):
                for b in range(KT):
                    n = g * (2 * KT) + N_FF + b
                    for i in range(2):
                        t = slice(i * HALF, (i + 1) * HALF)
                        u = g * (2 * KT) + 2 * b + i
                        dve.wait_ge(gemm_done, 2 * n + i + 1)
                        dve.scalar_tensor_tensor(ev[i][:], gp[i][:], 0.0, rstd1[:, t], ALU.max, ALU.mult).then_inc(gp_free, 1)
                        dve.wait_ge(gp_free, 2 * n + i + 1)
                        dve.sem_inc(z_ready, 1)
                        if first and b + i == 0:
                            norm_factor(1)
                        dve.wait_ge(u_hi, u + 1)
                        dve.tensor_tensor(r2l[:, b, t], ut[i][:], r2h[:, b, t].bitcast(F32), ALU.subtract).then_inc(u_lo, 1)

            def ff2(g):
                for k in range(KT):
                    n = g * (2 * KT) + N_FF + KT + k
                    for i in range(2):
                        t = slice(i * HALF, (i + 1) * HALF)
                        dve.wait_ge(gemm_done, 2 * n + i + 1)
                        dve.tensor_tensor(res[:, k, t], gp[i][:], res[:, k, t], ALU.add).then_inc(gp_free, 1)

            ff1(0, first=True)
            ff2(0)
            with dve.Fori(1, GROUPS - 1) as g:
                ff1(g)
                ff2(g)
            ff1(GROUPS - 1)

            def out_scale(half):
                r = rfin[:, 4 * half:4 * half + 4]
                dve.wait_ge(fs_done, half + 1)
                sums = tr[:, 16 * half:16 * half + 16].rearrange("p (t n) -> p t n", n=4)[:, :, 0]
                dve.tensor_scalar(r, sums, 1.0 / D, EPS, ALU.mult, ALU.add).then_inc(f_var, 1)
                dve.wait_ge(f_std, half + 1)
                dve.reciprocal(r, r).then_inc(f_rstd, 1)
                dve.wait_ge(f_rstd, half + 1)

            def out_tile(t):
                banks = gp if t == 6 else [sbank[:, 2 * (t % 2 if t < 6 else 0) + i, :] for i in range(2)]
                if t >= 2:
                    dve.wait_ge(out_st[t % 2], 16 * (t // 2))
                for i in range(2):
                    cols = slice(i * HALF, (i + 1) * HALF)
                    dve.wait_ge(ft_tr, 2 * t + i + 1)
                    dve.scalar_tensor_tensor(otok[t % 2][:, cols], banks[i][:], rfin[:, t:t + 1], fnb[i][:],
                                             ALU.mult, ALU.mult).then_inc(ft_out, 1)

            for m in range(2 * KT):
                half, k = divmod(m, KT)
                n = N_LAST + m
                t = slice(half * HALF, (half + 1) * HALF)
                dve.wait_ge(gemm_done, 2 * n + 2)
                dve.tensor_tensor(res[:, k, t], gp[m % 2][:], res[:, k, t], ALU.add).then_inc(gp_free, 2)
                dve.wait_ge(gp_free, 2 * n + 2)
                dve.sem_inc(fin_done, 1)
                if half and k == 1:
                    out_scale(0)
                if half and 2 <= k < 6:
                    if k == 2:
                        dve.wait_ge(fnb_in, 32)
                    out_tile(k - 2)
            out_scale(1)
            for t in range(4, TT):
                out_tile(t)

        @block.gpsimd
        def _(pool):
            def split_lo(n, slot):
                pool.wait_ge(w_hi, n + 1)
                pool.tensor_tensor(wl[slot][:], raw[slot][:], wh[slot][:].bitcast(F32), ALU.subtract).then_inc(w_split, 1)

            def square_add(stage, k, half):
                pool.wait_ge(sq_ready, 2 * KT * stage + (2 * k + half if stage == 0 else half * KT + k) + 1)
                if k:
                    a = acc[:, half * HALF:(half + 1) * HALF]
                    done = 2 * (k - 2) + half + 1 if stage == 0 else (half + 2) * (KT - 1) + k - 1
                    if k > 1:
                        pool.wait_ge(sq_used, done)
                    pool.tensor_tensor(a, a, ut[half if stage == 0 else k % 2][:], ALU.add).then_inc(sq_used, 1)

            pool.memset(wifh[:].bitcast(F32), 0.0).then_inc(wif_set, 1)
            pool.memset(wifl[:].bitcast(F32), 0.0).then_inc(wif_set, 1)
            pool.dma_start(cosT[:].bitcast(I32), positions[0].partition_broadcast(P)).then_inc(c2_in, 16)
            pool.dma_start(inv[:], c_inv).then_inc(c2_in, 16)
            pool.dma_start(sg[:, 0:3 * P], c_mask).then_inc(c2_in, 16)
            pool.dma_start(keep[:], c_keep).then_inc(c2_in, 16)
            pool.wait_ge(wif_h, 2)
            pool.tensor_tensor(wifl[:, :, 0:NH], wif[:, :, 0:NH], wifh[:, :, 0:NH].bitcast(F32), ALU.subtract)
            pool.tensor_tensor(wifl[:, :, 32:32 + NH], wif[:, :, NH:2 * NH], wifh[:, :, 32:32 + NH].bitcast(F32),
                               ALU.subtract).then_inc(wif_l, 1)
            split_lo(0, 0)
            for b in range(HB):
                split_lo(b + 1, (b + 1) % 2)
            pool.wait_ge(c2_in, 16 * 4)
            pool.wait_ge(tk_done, 1)
            pool.wait_ge(c_in, 16 * 19)

            def attend(h, s):
                if s == 2:
                    wait(pool, obt, 2 * h)
                    pool.tensor_copy(hk[:], tk[:, :, :, bass.ds(h, 1)].rearrange("p c q a -> p c (q a)")).then_inc(hk_ready, 1)
                    pool.tensor_copy(hd[:], dc[:, :, bass.ds(h, 1)].rearrange("p c a -> p (c a)")).then_inc(hk_ready, 1)
                    pool.tensor_copy(hc[:], cw[:, :, bass.ds(h, 1)].rearrange("p c a -> p (c a)")).then_inc(hk_ready, 1)
                    pool.tensor_copy(hw[:], mlw[:, bass.ds(h, 1)]).then_inc(hk_ready, 1)
                if s == 8:
                    pool.wait_ge(sg_ready, h + 1)
                    pool.tensor_tensor(kqs[:], kqs[:], sg[:], ALU.mult).then_inc(kq_ready, 1)
                if s == 12:
                    pool.wait_ge(st_done, h + 1)
                    pool.wait_ge(i_in, 16 * h + 16)
                    pool.tensor_tensor(qpad[0:DK, :], qpad[0:DK, :], kraw[0:DK, :], ALU.mult).then_inc(qi_ready, 1)

            def head_round(h, att):
                for s in range(SLOTS):
                    for k in STARTS_AT[s]:
                        if k % 2:
                            continue
                        split_lo(h * HB + k // 2 + 1, (k // 2 + 1) % 2)
                    attend(att, s)

            head_round(1, 0)
            with pool.Fori(2, NH) as h:
                head_round(h, h - 1)
            for s in range(SLOTS):
                for k in GATE_UNITS_AT[s]:
                    n = N_GATE + k // 2
                    if k % 2 == 0:
                        split_lo(n + 1, (n + 1) % 2)
                attend(NH - 1, s)
            for j in range(12, 16):
                n = N_GATE + j
                split_lo(n + 1, (n + 1) % 2)

            def stage_lo(k, hi, lo):
                pool.wait_ge(stg_hi, k + 1)
                pool.tensor_tensor(lo[:, k % KT, :], stg[k % 2][:], hi[:, k % KT, :].bitcast(F32), ALU.subtract).then_inc(stgb_lo, 1)

            for j in range(2 * KT):
                n = N_PA + j
                split_lo(n + 1, (n + 1) % 2)
                if j < KT:
                    stage_lo(KT + j, r1h, r1l)
                else:
                    for i in range(2):
                        k = j - KT
                        t = slice(i * HALF, (i + 1) * HALF)
                        pool.wait_ge(m_hi, 2 * k + i + 1)
                        pool.tensor_tensor(r2l[:, k, t], ev[i][:], r2h[:, k, t].bitcast(F32), ALU.subtract).then_inc(m_lo, 1)
            for k in range(KT):
                n = N_WO + k
                split_lo(n + 1, (n + 1) % 2)
                for i in range(2):
                    square_add(0, k, i)

            with pool.Fori(0, GROUPS - 1) as g:
                for b in range(2 * KT):
                    split_lo(g * (2 * KT) + N_FF + b + 1, (b + 1) % 2)
            for b in range(KT):
                split_lo((GROUPS - 1) * 2 * KT + N_FF + b + 1, (b + 1) % 2)
            for m in range(2 * KT):
                if m < 2 * KT - 1:
                    split_lo(N_LAST + m + 1, (m + 1) % 2)
                half, k = divmod(m, KT)
                square_add(1, k, half)


def shape_constants():
    inv = (500000.0 ** (-np.arange(0, 16, 2, dtype=np.float32) / 16)).astype(np.float32)
    col = np.zeros((P, 1), np.float32)
    for base in (0, DK):
        col[base:base + 8, 0] = -inv
        col[base + 8:base + 16, 0] = inv
    mask = np.zeros((P, 3 * P), np.float32)
    mask[:, P:2 * P][np.arange(P)[None, :] > np.arange(P)[:, None]] = NEG
    last = np.zeros((P, P), np.float32)
    last[P - 1, :] = 1.0
    carry = np.ones((NH, S), np.float32)
    carry[:, ::P] = 0.0
    keep = np.where(np.arange(P)[None, :] >= np.arange(P)[:, None], np.float32(3e38), np.float32(0))
    return {"c_ident": np.eye(P, dtype=np.float32), "c_inv": col, "c_mask": mask,
            "c_last": last, "c_carry": carry, "c_keep": keep}


_INS = ["x", "positions", "norm_mix_w", "w_in", "ml_gate_b", "conv_w", "conv_b", "da_lambda", "da_subln_w",
        "ml_norm_w", "w_proj_a", "w_proj_b", "w_out", "norm_ffn_w", "w_ff1", "w_ff2", "final_norm_w"]
_CONSTS = ["c_ident", "c_inv", "c_mask", "c_last", "c_carry", "c_keep"]


def kernel(**inputs):
    import concourse.bacc as _bacc
    from concourse.bass_utils import run_bass_kernel_spmd as _run

    nc = _bacc.Bacc("TRN2", target_bir_lowering=False, num_devices=1)
    arrays, args = {}, []
    consts = shape_constants()
    for name in _INS + _CONSTS:
        a = np.ascontiguousarray(consts[name] if name in consts else inputs[name])
        arrays[f"in_{name}"] = a
        args.append(nc.dram_tensor(f"in_{name}", a.shape, mybir.dt.from_np(a.dtype), kind="ExternalInput").ap())
    out = nc.dram_tensor("out_0", (1, S, D), F32, kind="ExternalOutput").ap()
    build(nc, *args, out)
    r = _run(nc, [arrays], core_ids=[0])
    return r.results[0]["out_0"]
```
